# Optimizing a Trainium2 kernel written in Bass

```python
import math
import jax
import jax.numpy as jnp
from jax import lax
import numpy as np
import jax, jax.numpy as jnp

D_MODEL = 1024
BATCH = 1
SEQ = 256
DEPTH = 2

ROPE_THETA = 10000.0
NORM_EPS = 1e-6
QBLK = 128
NEG = -1e30

A_HEADS = 6
A_HEAD_DIM = 64
A_CONFIGS = ((128, 1), (512, 4), (2048, 16))
B_HEADS = 6
B_NOPE = 64
B_ROPE = 32
B_V = 64
B_Q_LORA = 384
B_KV_LORA = 128
C_HEADS = 4
C_QK = 32
C_V = 2 * C_QK
C_SUBLN_EPS = 1e-5

A_WIDTH = A_HEADS * A_HEAD_DIM
B_WIDTH = B_HEADS * B_V
C_WIDTH = C_HEADS * C_V
MIX_WIDTH = A_WIDTH + B_WIDTH + C_WIDTH

IN_SPLITS = (A_WIDTH, A_WIDTH, A_WIDTH,
             B_Q_LORA, B_KV_LORA, B_ROPE,
             C_HEADS * 2 * C_QK, C_HEADS * 2 * C_QK, C_WIDTH)
IN_COLS = int(sum(IN_SPLITS))
D_FF = 4 * D_MODEL


def rmsnorm(x, g, eps=NORM_EPS):
    xf = x.astype(jnp.float32)
    y = xf * lax.rsqrt(jnp.mean(xf * xf, axis=-1, keepdims=True) + eps)
    return (y * g.astype(jnp.float32)).astype(x.dtype)

def rope_tables(seq, dim):
    half = dim // 2
    inv = 1.0 / (ROPE_THETA ** (jnp.arange(half, dtype=jnp.float32) / half))
    ang = jnp.arange(seq, dtype=jnp.float32)[:, None] * inv[None, :]
    return jnp.cos(ang), jnp.sin(ang)

def apply_rope(x, cos, sin):
    half = x.shape[-1] // 2
    xf = x.astype(jnp.float32)
    x1, x2 = xf[..., :half], xf[..., half:]
    return jnp.concatenate([x1 * cos - x2 * sin, x1 * sin + x2 * cos], axis=-1).astype(x.dtype)

def to_heads(t, n_heads):
    b, s, _ = t.shape
    return t.reshape(b, s, n_heads, -1).transpose(0, 2, 1, 3)

def from_heads(t):
    b, h, s, d = t.shape
    return t.transpose(0, 2, 1, 3).reshape(b, s, h * d)

def banded_attn(q, k, v, span, scale):
    b, g, n, dh = q.shape
    nb = n // span
    qb = q.reshape(b, g, nb, span, dh)
    kb = k.reshape(b, g, nb, span, dh)
    vb = v.reshape(b, g, nb, span, v.shape[-1])

    def with_prev(t):
        prev = jnp.pad(t[:, :, :-1], ((0, 0), (0, 0), (1, 0), (0, 0), (0, 0)))
        return jnp.concatenate([prev, t], axis=3)

    kk, vv = with_prev(kb), with_prev(vb)
    s = jnp.einsum('bgnqd,bgnkd->bgnqk', qb, kk).astype(jnp.float32) * scale
    qi = jnp.arange(span)[:, None]
    ki = jnp.arange(2 * span)[None, :]
    dist = qi + span - ki
    blk = jnp.arange(nb)[:, None, None]
    valid = (dist >= 0) & (dist <= span) & ((blk > 0) | (ki >= span))
    s = jnp.where(valid, s, NEG)
    lse = jax.nn.logsumexp(s, axis=-1)
    p = jnp.exp(s - lse[..., None])
    out = jnp.einsum('bgnqk,bgnkd->bgnqd', p.astype(v.dtype), vv)
    return out.reshape(b, g, n, -1), lse.reshape(b, g, n)

def dilated_attn(q, k, v, window, dilation, scale):
    b, h, s, dh = q.shape
    span = window // dilation
    unit = dilation * span
    sp = -(-s // unit) * unit
    sub = sp // dilation

    def split(t):
        t = jnp.pad(t, ((0, 0), (0, 0), (0, sp - s), (0, 0)))
        return t.reshape(b, h, sub, dilation, t.shape[-1]).transpose(0, 1, 3, 2, 4).reshape(b, h * dilation, sub, t.shape[-1])

    out, lse = banded_attn(split(q), split(k), split(v), span, scale)
    out = out.reshape(b, h, dilation, sub, -1).transpose(0, 1, 3, 2, 4).reshape(b, h, sp, -1)[:, :, :s]
    lse = lse.reshape(b, h, dilation, sub).transpose(0, 1, 3, 2).reshape(b, h, sp)[:, :, :s]
    return out, lse

def causal_attn(q, k, v, scale, coef):
    b, h, m, s, dq = q.shape
    nb = s // QBLK
    qb = q.reshape(b, h, m, nb, QBLK, dq).transpose(3, 0, 1, 2, 4, 5)
    kpos = jnp.arange(s)

    def one(args):
        qblk, i = args
        sc = jnp.einsum('bhmqd,bhmkd->bhmqk', qblk, k).astype(jnp.float32) * scale
        qpos = i * QBLK + jnp.arange(QBLK)
        sc = jnp.where(kpos[None, :] <= qpos[:, None], sc, NEG)
        p = jnp.einsum('bhmqk,m->bhqk', jax.nn.softmax(sc, axis=-1), coef)
        return jnp.einsum('bhqk,bhkd->bhqd', p.astype(v.dtype), v)

    out = lax.map(one, (qb, jnp.arange(nb)))
    return out.transpose(1, 2, 0, 3, 4).reshape(b, h, s, -1)

def mixer_dilated(qa, ka, va, cos64, sin64):
    q = apply_rope(to_heads(qa, A_HEADS), cos64, sin64)
    k = apply_rope(to_heads(ka, A_HEADS), cos64, sin64)
    v = to_heads(va, A_HEADS)
    scale = A_HEAD_DIM ** -0.5
    outs, lses = [], []
    for window, dilation in A_CONFIGS:
        o, l = dilated_attn(q, k, v, window, dilation, scale)
        outs.append(o)
        lses.append(l)
    w = jax.nn.softmax(jnp.stack(lses, axis=0), axis=0)
    out = jnp.sum(w[..., None].astype(v.dtype) * jnp.stack(outs, axis=0), axis=0)
    return from_heads(out)

def mixer_mla(cq, ckv, kr, q_norm_g, w_uq, kv_norm_g, w_ukv, cos32, sin32):
    b, s, _ = cq.shape
    qf = to_heads(rmsnorm(cq, q_norm_g) @ w_uq, B_HEADS)
    kvf = to_heads(rmsnorm(ckv, kv_norm_g) @ w_ukv, B_HEADS)
    q = jnp.concatenate([qf[..., :B_NOPE], apply_rope(qf[..., B_NOPE:], cos32, sin32)], axis=-1)
    k_rope = jnp.broadcast_to(apply_rope(kr, cos32, sin32)[:, None], (b, B_HEADS, s, B_ROPE))
    k = jnp.concatenate([kvf[..., :B_NOPE], k_rope], axis=-1)
    v = kvf[..., B_NOPE:]
    coef = jnp.ones((1,), jnp.float32)
    out = causal_attn(q[:, :, None], k[:, :, None], v, (B_NOPE + B_ROPE) ** -0.5, coef)
    return from_heads(out)

def mixer_diff(qc, kc, vc, lam_params, subln_g, lam_init, cos32, sin32):
    b, s, _ = qc.shape
    q = apply_rope(qc.reshape(b, s, C_HEADS, 2, C_QK).transpose(0, 2, 3, 1, 4), cos32, sin32)
    k = apply_rope(kc.reshape(b, s, C_HEADS, 2, C_QK).transpose(0, 2, 3, 1, 4), cos32, sin32)
    v = to_heads(vc, C_HEADS)
    lp = lam_params.astype(jnp.float32)
    lam = jnp.exp(jnp.sum(lp[0] * lp[1])) - jnp.exp(jnp.sum(lp[2] * lp[3])) + lam_init
    coef = jnp.stack([jnp.ones((), jnp.float32), -lam])
    out = causal_attn(q, k, v, C_QK ** -0.5, coef)
    out = rmsnorm(out, subln_g, C_SUBLN_EPS) * (1.0 - lam_init)
    return from_heads(out)

def first_inputs(seed: int = 0) -> dict:
    key = jax.random.key(seed)
    ks = jax.random.split(key, 16)

    def nrm(k, shape, fan):
        return jax.random.normal(k, shape, jnp.float32) * (fan ** -0.5)

    def gain(k, shape):
        return 1.0 + 0.02 * jax.random.normal(k, shape, jnp.float32)

    return {
        "x": jax.random.normal(ks[0], (BATCH, SEQ, D_MODEL), jnp.float32),
        "ln1_g": gain(ks[1], (DEPTH, D_MODEL)),
        "w_in": nrm(ks[2], (DEPTH, D_MODEL, IN_COLS), D_MODEL),
        "mla_q_norm_g": gain(ks[3], (DEPTH, B_Q_LORA)),
        "mla_w_uq": nrm(ks[4], (DEPTH, B_Q_LORA, B_HEADS * (B_NOPE + B_ROPE)), B_Q_LORA),
        "mla_kv_norm_g": gain(ks[5], (DEPTH, B_KV_LORA)),
        "mla_w_ukv": nrm(ks[6], (DEPTH, B_KV_LORA, B_HEADS * (B_NOPE + B_V)), B_KV_LORA),
        "diff_lambda": 0.1 * jax.random.normal(ks[7], (DEPTH, 4, C_QK), jnp.float32),
        "diff_subln_g": gain(ks[8], (DEPTH, C_V)),
        "w_o": nrm(ks[9], (DEPTH, MIX_WIDTH, D_MODEL), MIX_WIDTH),
        "ln2_g": gain(ks[10], (DEPTH, D_MODEL)),
        "w_up": nrm(ks[11], (DEPTH, D_MODEL, D_FF), D_MODEL),
        "w_down": nrm(ks[12], (DEPTH, D_FF, D_MODEL), D_FF),
        "final_g": gain(ks[13], (D_MODEL,)),
    }

def first_block(x, ln1_g, w_in, mla_q_norm_g, mla_w_uq, mla_kv_norm_g, mla_w_ukv,
              diff_lambda, diff_subln_g, w_o, ln2_g, w_up, w_down, final_g):
    s = x.shape[1]
    cos64, sin64 = rope_tables(s, A_HEAD_DIM)
    cos32, sin32 = rope_tables(s, C_QK)
    split_idx = [int(v) for v in np.cumsum(IN_SPLITS)[:-1]]

    for layer in range(DEPTH):
        lam_init = 0.8 - 0.6 * math.exp(-0.3 * layer)
        h = rmsnorm(x, ln1_g[layer])
        proj = h @ w_in[layer]
        qa, ka, va, cq, ckv, kr, qc, kc, vc = jnp.split(proj, split_idx, axis=-1)

        out_a = mixer_dilated(qa, ka, va, cos64, sin64)
        out_b = mixer_mla(cq, ckv, kr, mla_q_norm_g[layer], mla_w_uq[layer],
                          mla_kv_norm_g[layer], mla_w_ukv[layer], cos32, sin32)
        out_c = mixer_diff(qc, kc, vc, diff_lambda[layer], diff_subln_g[layer], lam_init, cos32, sin32)

        mixed = jnp.concatenate([out_a, out_b, out_c], axis=-1)
        x = x + mixed @ w_o[layer]

        u = rmsnorm(x, ln2_g[layer]) @ w_up[layer]
        x = x + jnp.square(jax.nn.relu(u)) @ w_down[layer]

    return rmsnorm(x, final_g)


DEPTH_2 = 4

N_MIXERS = 3
N_RET = len(range(0, DEPTH_2, N_MIXERS))
N_CF = len(range(1, DEPTH_2, N_MIXERS))
N_SC = len(range(2, DEPTH_2, N_MIXERS))
RET_HEADS = 4
RET_DK = D_MODEL // RET_HEADS
RET_VDIM = 2 * D_MODEL
RET_DV = RET_VDIM // RET_HEADS
RET_CHUNK = 128
RET_IN = 2 * D_MODEL + 2 * RET_VDIM
ROPE_BASE = 10000.0
CF_KERNEL = 31
SC_KERNEL = 3
D_FF_2 = 4 * D_MODEL
RMS_EPS = 1e-6
LN_EPS = 1e-5


F32 = jnp.float32

def rms_norm(x, g):
    xf = x.astype(F32)
    y = xf * lax.rsqrt(jnp.mean(xf * xf, axis=-1, keepdims=True) + RMS_EPS)
    return (y * g.astype(F32)).astype(x.dtype)

def causal_depthwise_conv(x, w):
    k = w.shape[0]
    return lax.conv_general_dilated(
        x, w[:, None, :].astype(x.dtype), window_strides=(1,),
        padding=[(k - 1, 0)], dimension_numbers=("NWC", "WIO", "NWC"),
        feature_group_count=x.shape[-1])

def apply_rotary(t, cos, sin):
    t1, t2 = jnp.split(t, 2, axis=-1)
    return jnp.concatenate([t1 * cos - t2 * sin, t2 * cos + t1 * sin], axis=-1)

def chunkwise_retention(q, k, v):
    bsz, s, h, dk = q.shape
    dv = v.shape[-1]
    nc = s // RET_CHUNK
    log_gamma = jnp.log1p(-jnp.exp2(-5.0 - jnp.arange(h, dtype=F32)))
    idx = jnp.arange(RET_CHUNK, dtype=F32)
    rel = idx[:, None] - idx[None, :]
    intra = jnp.where(rel >= 0, jnp.exp(log_gamma[:, None, None] * jnp.maximum(rel, 0.0)), 0.0)
    q_decay = jnp.exp(log_gamma[:, None] * (idx + 1.0))
    k_decay = jnp.exp(log_gamma[:, None] * (RET_CHUNK - 1.0 - idx))
    chunk_decay = jnp.exp(log_gamma * RET_CHUNK)

    def to_chunks(t):
        return t.reshape(bsz, nc, RET_CHUNK, h, t.shape[-1]).transpose(1, 0, 3, 2, 4)

    def step(state, qkv):
        qc, kc, vc = qkv
        scores = jnp.einsum("bhid,bhjd->bhij", qc, kc) * intra
        out = (jnp.einsum("bhij,bhjv->bhiv", scores, vc)
               + jnp.einsum("bhid,bhdv->bhiv", qc * q_decay[..., None], state))
        state = (state * chunk_decay[:, None, None]
                 + jnp.einsum("bhjd,bhjv->bhdv", kc * k_decay[..., None], vc))
        return state, out

    state0 = jnp.zeros((bsz, h, dk, dv), F32)
    _, ys = lax.scan(step, state0, (to_chunks(q), to_chunks(k), to_chunks(v)))
    return ys.transpose(1, 0, 3, 2, 4).reshape(bsz, s, h, dv)

def retention_mixer(x, positions, w_in, gn_g, w_out):
    bsz, s, _ = x.shape
    proj = x @ w_in
    q, k, v, g = jnp.split(proj, [D_MODEL, 2 * D_MODEL, 2 * D_MODEL + RET_VDIM], axis=-1)
    q = q.reshape(bsz, s, RET_HEADS, RET_DK).astype(F32)
    k = k.reshape(bsz, s, RET_HEADS, RET_DK).astype(F32)
    v = v.reshape(bsz, s, RET_HEADS, RET_DV).astype(F32)
    inv_freq = ROPE_BASE ** (-jnp.arange(0, RET_DK, 2, dtype=F32) / RET_DK)
    ang = positions.astype(F32)[..., None, None] * inv_freq
    cos, sin = jnp.cos(ang), jnp.sin(ang)
    q = apply_rotary(q, cos, sin)
    k = apply_rotary(k, cos, sin) * (RET_DK ** -0.5)
    y = chunkwise_retention(q, k, v)
    mean = jnp.mean(y, axis=-1, keepdims=True)
    var = jnp.mean(jnp.square(y - mean), axis=-1, keepdims=True)
    y = ((y - mean) * lax.rsqrt(var + LN_EPS)).reshape(bsz, s, RET_VDIM) * gn_g.astype(F32)
    y = (jax.nn.silu(g.astype(F32)) * y).astype(x.dtype)
    return y @ w_out

def conformer_conv_mixer(x, w_pw1, b_pw1, w_dw, b_dw, ln_g, ln_b, w_pw2, b_pw2):
    h = x @ w_pw1 + b_pw1
    a, gate = jnp.split(h, 2, axis=-1)
    h = a * jax.nn.sigmoid(gate)
    h = causal_depthwise_conv(h, w_dw) + b_dw
    hf = h.astype(F32)
    mean = jnp.mean(hf, axis=-1, keepdims=True)
    var = jnp.mean(jnp.square(hf - mean), axis=-1, keepdims=True)
    hf = (hf - mean) * lax.rsqrt(var + LN_EPS) * ln_g.astype(F32) + ln_b.astype(F32)
    h = jax.nn.silu(hf).astype(x.dtype)
    return h @ w_pw2 + b_pw2

def short_conv_mixer(x, w_in, w_conv, w_out):
    gb, gc, h = jnp.split(x @ w_in, 3, axis=-1)
    u = causal_depthwise_conv(gc * h, w_conv)
    return (gb * u) @ w_out

def squared_relu_mlp(x, w1, w2):
    return jnp.square(jax.nn.relu(x @ w1)) @ w2

def second_inputs(seed: int = 0) -> dict:
    key = jax.random.key(seed)
    ks = iter(jax.random.split(key, 32))

    def dense(shape, fan_in):
        return jax.random.normal(next(ks), shape, F32) * (fan_in ** -0.5)

    def small(shape, scale):
        return jax.random.normal(next(ks), shape, F32) * scale

    x = jax.random.normal(next(ks), (BATCH, SEQ, D_MODEL), F32)
    positions = jnp.broadcast_to(jnp.arange(SEQ, dtype=jnp.int32), (BATCH, SEQ))
    return {
        "x": x,
        "positions": positions,
        "norm_g": 1.0 + small((DEPTH_2, 4, D_MODEL), 0.05),
        "ret_w_in": dense((N_RET, D_MODEL, RET_IN), D_MODEL),
        "ret_gn_g": 1.0 + small((N_RET, RET_VDIM), 0.05),
        "ret_w_out": dense((N_RET, RET_VDIM, D_MODEL), RET_VDIM),
        "cf_w_pw1": dense((N_CF, D_MODEL, 2 * D_MODEL), D_MODEL),
        "cf_b_pw1": small((N_CF, 2 * D_MODEL), 0.01),
        "cf_w_dw": dense((N_CF, CF_KERNEL, D_MODEL), CF_KERNEL),
        "cf_b_dw": small((N_CF, D_MODEL), 0.01),
        "cf_ln_g": 1.0 + small((N_CF, D_MODEL), 0.05),
        "cf_ln_b": small((N_CF, D_MODEL), 0.01),
        "cf_w_pw2": dense((N_CF, D_MODEL, D_MODEL), D_MODEL),
        "cf_b_pw2": small((N_CF, D_MODEL), 0.01),
        "sc_w_in": dense((N_SC, D_MODEL, 3 * D_MODEL), D_MODEL),
        "sc_w_conv": dense((N_SC, SC_KERNEL, D_MODEL), SC_KERNEL),
        "sc_w_out": dense((N_SC, D_MODEL, D_MODEL), D_MODEL),
        "mlp_w1": dense((DEPTH_2, D_MODEL, D_FF_2), D_MODEL),
        "mlp_w2": dense((DEPTH_2, D_FF_2, D_MODEL), D_FF_2),
    }

def second_block(x, positions, norm_g, ret_w_in, ret_gn_g, ret_w_out,
              cf_w_pw1, cf_b_pw1, cf_w_dw, cf_b_dw, cf_ln_g, cf_ln_b, cf_w_pw2, cf_b_pw2,
              sc_w_in, sc_w_conv, sc_w_out, mlp_w1, mlp_w2):
    for i in range(DEPTH_2):
        kind, j = i % N_MIXERS, i // N_MIXERS
        h = rms_norm(x, norm_g[i, 0])
        if kind == 0:
            h = retention_mixer(h, positions, ret_w_in[j], ret_gn_g[j], ret_w_out[j])
        elif kind == 1:
            h = conformer_conv_mixer(h, cf_w_pw1[j], cf_b_pw1[j], cf_w_dw[j], cf_b_dw[j],
                                     cf_ln_g[j], cf_ln_b[j], cf_w_pw2[j], cf_b_pw2[j])
        else:
            h = short_conv_mixer(h, sc_w_in[j], sc_w_conv[j], sc_w_out[j])
        x = x + rms_norm(h, norm_g[i, 1])
        h = squared_relu_mlp(rms_norm(x, norm_g[i, 2]), mlp_w1[i], mlp_w2[i])
        x = x + rms_norm(h, norm_g[i, 3])
    return x


def setup_inputs(seed=0):
    out = dict(first_inputs(seed))
    for name, value in second_inputs(seed + 1).items():
        if name != "x":
            out[name + "_2"] = value
    return out


def reference(
    x, ln1_g, w_in, mla_q_norm_g, mla_w_uq, mla_kv_norm_g, mla_w_ukv, diff_lambda, diff_subln_g,
    w_o, ln2_g, w_up, w_down, final_g, positions_2, norm_g_2, ret_w_in_2, ret_gn_g_2,
    ret_w_out_2, cf_w_pw1_2, cf_b_pw1_2, cf_w_dw_2, cf_b_dw_2, cf_ln_g_2, cf_ln_b_2, cf_w_pw2_2,
    cf_b_pw2_2, sc_w_in_2, sc_w_conv_2, sc_w_out_2, mlp_w1_2, mlp_w2_2,
):
    x = first_block(
        x, ln1_g, w_in, mla_q_norm_g, mla_w_uq, mla_kv_norm_g, mla_w_ukv, diff_lambda,
        diff_subln_g, w_o, ln2_g, w_up, w_down, final_g,
    )
    return second_block(
        x, positions_2, norm_g_2, ret_w_in_2, ret_gn_g_2, ret_w_out_2, cf_w_pw1_2, cf_b_pw1_2,
        cf_w_dw_2, cf_b_dw_2, cf_ln_g_2, cf_ln_b_2, cf_w_pw2_2, cf_b_pw2_2, sc_w_in_2,
        sc_w_conv_2, sc_w_out_2, mlp_w1_2, mlp_w2_2,
    )


_drawn_inputs = setup_inputs


def setup_inputs(seed=0):
    import zlib

    import numpy as np

    out = dict(_drawn_inputs(seed))
    spreads = {}
    factors = {'mla_q_norm_g': 7.759,
     'mla_kv_norm_g': 3.167,
     'cf_b_pw1_2': 6.71,
     'cf_b_dw_2': 3.241,
     'cf_ln_b_2': 7.594,
     'cf_b_pw2_2': 4.181}
    for name, (base, spread) in spreads.items():
        noise = np.random.default_rng([zlib.crc32(name.encode()), seed]).standard_normal(out[name].shape)
        drawn = base * np.exp(spread * noise) if base else spread * noise
        out[name] = jnp.asarray(drawn.astype(out[name].dtype))
    for name, factor in factors.items():
        out[name] = (out[name] * factor).astype(out[name].dtype)
    return out
```

```python
from contextlib import ExitStack
import math

import concourse.bass as bass
from concourse import mybir

F32 = mybir.dt.float32
F32R = mybir.dt.float32r
I32 = mybir.dt.int32
ALU = mybir.AluOpType
ACT = mybir.ActivationFunctionType
AX = mybir.AxisListType

P = 128
D = 1024
S = 256
NT = S // P
KC = D // P
FF = 4 * D
DEPTH1, DEPTH2 = 2, 4
AH, AD = 6, 64
BH, BN, BR, BV = 6, 64, 32, 64
BQ, BKV = 384, 128
CH, CQ, CV = 4, 32, 64
IN_COLS = 3 * AH * AD + BQ + BKV + BR + 2 * CH * 2 * CQ + CH * CV
QA, KA, VA = 0, AH * AD, 2 * AH * AD
CQ0 = 3 * AH * AD
CKV0 = CQ0 + BQ
KR0 = CKV0 + BKV
QC0 = KR0 + BR
KC0 = QC0 + 2 * CH * CQ
VC0 = KC0 + 2 * CH * CQ
RH, RDK, RDV = 4, 256, 512
CFK, SCK = 31, 3
EPS, SUB_EPS, LN_EPS = 1e-6, 1e-5, 1e-5
BQD = BN + BR

RING = 4
AHEAD = 3
TW = 2048
STEPS = FF // 256
LOOPS = (STEPS - 4) // 2

ROWS = {}
_n = 0
for _name, _count in (("ln1", 2), ("ln2", 2), ("norm", 16), ("gn", 4), ("bpw1", 2), ("wdw", CFK), ("bdw", 1),
                      ("lng", 1), ("lnb", 1), ("wconv", SCK), ("qn", 2), ("kvn", 2)):
    ROWS[_name] = _n
    _n += _count
N_ROWS = _n
ROWS_AT = [N_ROWS if c == 0 else ROWS["kvn"] if c < BQ // P else ROWS["qn"] for c in range(KC)]

TWO_PI_PARTS = (6.28125, 0.00193500518798828125, 3.0199159795e-07)
PI_BELOW = 3.1415925

SECTIONS = ([("attn", 0), ("mlp1", 0), ("attn", 1), ("mlp1", 1), ("fin", 0)]
            + [(k, i) for i, m in enumerate(("ret", "cf", "sc", "ret")) for k in (m, "mlp2")])
TILES = {"attn": 16, "mlp1": 32, "mlp2": 32, "fin": 0, "ret": 32, "cf": 12, "sc": 16}
MAPS = AH + BH + 2 * CH
SC_UP = (0, 3, 7, 11)
SC_OUT = (6, 10, 14, 15)

FEED = dict(attn=1, mlp1=1, mlp2=1, ret=1, cf=1, sc=1)


def times(n, kinds):
    return {k: n for k in kinds.split()}


ALL = "attn mlp1 mlp2 ret cf sc"
POST = "mlp2 ret cf sc"
class Section:
    def __init__(self, index):
        self.kind, self.layer = SECTIONS[index]
        self.index = index
        self.tile0 = sum(TILES[k] for k, _ in SECTIONS[:index])
        self.tiles = TILES[self.kind]

    def slot(self, c):
        return (self.tile0 + c) % RING

    def fill(self, c, i=0):
        return i + (self.tile0 + c) // RING


class Stage:

    def __init__(self, sem, incs):
        self.sem = sem
        self.base = [sum(incs.get(k, 0) for k, _ in SECTIONS[:i]) for i in range(len(SECTIONS) + 1)]

    def at(self, sec, n):
        v = n + self.base[sec.index]
        return max(v, 0) if isinstance(v, int) else v


class Chain:

    def __init__(self, eng, sem):
        self.eng, self.sem, self.n = eng, sem, 0

    def mark(self, ins):
        ins.then_inc(self.sem, 1)
        self.n += 1
        return self.n

    def link(self, ins):
        self.eng.wait_ge(self.sem, self.mark(ins))


N_TILES = sum(TILES[k] for k, _ in SECTIONS)


def owner(t):
    for i in range(len(SECTIONS)):
        sec = Section(i)
        if t < sec.tile0 + sec.tiles:
            return "vector" if sec.kind.startswith("mlp") and t % 2 == 0 else "gpsimd"


def build(nc, a, out):
    ctx = ExitStack()
    with ctx:
        def sb(name, shape, dt=F32):
            return ctx.enter_context(nc.sbuf_tensor(name, shape, dt))

        def sem(name):
            return ctx.enter_context(nc.semaphore(name))

        w_raw = sb("w_raw", [P, RING, TW])
        w_hi = sb("w_hi", [P, RING, TW], F32R)
        w_lo = sb("w_lo", [P, RING, TW], F32R)
        x = sb("x_res", [P, NT, D])
        xT_h = sb("xT_h", [P, KC, S], F32R)
        xT_l = sb("xT_l", [P, KC, S], F32R)
        u_h = sb("u_h", [P, 2, 2, S], F32R)
        u_l = sb("u_l", [P, 2, 2, S], F32R)
        arena = sb("arena", [P, 16384])
        ident = sb("ident", [P, P])
        rope = sb("rope", [P, NT, 96])
        masks = sb("masks", [P, 2, 384])
        gcol = sb("gcol", [P, KC, N_ROWS])
        row = sb("row", [P, D])
        cs = sb("cs", [P, NT, 2, 128])
        lam_rows = sb("lam_rows", [P, DEPTH1, 4 * CQ])
        sub_g = sb("sub_g", [P, DEPTH1, CV])
        st = sb("st", [P, 96])
        pos_i = sb("pos_i", [P, NT], I32)
        ps = ctx.enter_context(nc.psum_tensor("ps", [P, 8, 512], F32))

        def region(start, *shape):
            n = math.prod(shape)
            v = arena[:, start:start + n]
            if len(shape) == 2:
                return v.rearrange("p (a b) -> p a b", a=shape[0])
            if len(shape) == 3:
                return v.rearrange("p (a b c) -> p a b c", a=shape[0], b=shape[1])
            return v

        junk = region(14336, 1024)
        tmp = region(15360, 1024)
        rows = region(0, 1024)
        s_ang, s_n, s_r, s_inv = region(1024, NT, 128), region(1280, NT, 128), region(1536, NT, 128), region(1792, 128)
        pr = region(0, NT, IN_COLS)
        o = NT * IN_COLS
        qb = region(o, NT, BH, BQD)
        kb = region(o + NT * BH * BQD, NT, BH, BQD)
        vb = region(o + 2 * NT * BH * BQD, NT, BH, BV)
        mixed = region(8000, NT, D)
        qkT = region(10048, 2, 512)
        sm = region(11072, 2, 384)
        pT = region(11840, 2, 384)
        rope_a, rope_b = region(12608, 768), region(13376, 768)
        relu = region(1024, 2, 512)
        sq = region(2048, 2, 512)
        rqk = region(0, NT, 2048)
        rv = region(4096, NT, 2048)
        rqkT = region(8192, 16, S)
        rg = region(12288, NT, 2048)
        rST = region(0, RH, 384)
        rD = region(1536, RH, 384)
        ry = region(8192, NT, 2048)
        rope_ra = [region(8192 + 2048 * i, 8, 128) for i in range(2)]
        rope_rb = [region(8192 + 2048 * i + 1024, 8, 128) for i in range(2)]
        xn = region(0, NT, D)
        cz = region(2048, KC, CFK - 1 + S)
        csg = region(4352, 2, 2, S)
        ccv = region(5376, KC, S)
        ch = region(7424, NT, D)
        csl = region(9472, 2, 2, S)
        cbias = region(10496, D)
        chh = region(11520, NT, D)
        sgb, sgc = region(2048, 2, 2, S), region(3072, 2, 2, S)
        sz = region(4096, 2, 2 * (S + SCK - 1)).rearrange("p a (c n) -> p a c n", c=2)
        scv = region(5248, 2, S)
        sy = region(5760, 2, 2, S)

        ss, ms, rstd, r2 = st[:, 0:2], st[:, 2:4], st[:, 4:6], st[:, 6:8]
        pss, pms, prs, coef = st[:, 8:10], st[:, 10:12], st[:, 12:14], st[:, 14:16]
        lss, lms, lrs = st[:, 16:20], st[:, 20:24], st[:, 24:28]
        negmax, zsum, rz = st[:, 28:32], st[:, 32:36], st[:, 36:40]
        sss, sms, srs = st[:, 40:48], st[:, 48:56], st[:, 56:64]
        lam4, lexp, neglam = st[:, 64:68], st[:, 68:72], st[:, 72:74]
        posf = st[:, 74:76]
        mv = sb("mv", [P, RH * NT, 2])
        gvar, grs, gshift = sb("gvar", [P, 8]), sb("grs", [P, 8]), sb("gshift", [P, 8])
        bns = sb("bns", [P, 4, 6])
        mhalf = sb("mhalf", [P, 8])

        raw_in = [sem(f"raw_in{i}") for i in range(RING)]
        hi_ready = [sem(f"hi_ready{i}") for i in range(RING)]
        lo_ready = [sem(f"lo_ready{i}") for i in range(RING)]
        used = [sem(f"used{i}") for i in range(RING)]
        x_ready = Stage(sem("x_ready"), times(2, ALL + " fin"))
        ss_ready = Stage(sem("ss_ready"), times(1, ALL + " fin"))
        rstd_ready = Stage(sem("rstd_ready"), times(1, ALL + " fin"))
        xn_ready = Stage(sem("xn_ready"), times(1, "cf sc"))
        xT_ready = Stage(sem("xT_ready"), times(4, ALL))
        xT_hi = Stage(sem("xT_hi"), times(8, ALL))
        xT_lo = Stage(sem("xT_lo"), times(8, ALL))
        evac_a = Stage(sem("evac_a"), {"attn": 5, "ret": 12})
        evac_v = Stage(sem("evac_v"), {"attn": 5, "ret": 8})
        feed_T = Stage(sem("feed_T"), {"attn": 4, "ret": 8, "cf": 4})
        feed_hi = Stage(sem("feed_hi"), {"attn": 4, "mlp1": 16, "mlp2": 16, "ret": 8, "cf": 4, "sc": 4})
        feed_lo = Stage(sem("feed_lo"), {"attn": 4, "mlp1": 16, "mlp2": 16, "ret": 8, "cf": 4, "sc": 4})
        row_in = Stage(sem("row_in"), times(16, POST + " fin"))
        post_ss = Stage(sem("post_ss"), times(2, POST))
        post_rs = Stage(sem("post_rs"), times(2, POST))
        relu_done = Stage(sem("relu_done"), {"mlp1": 16, "mlp2": 16})
        sq_done = Stage(sem("sq_done"), {"mlp1": 16, "mlp2": 16})
        lat_T = Stage(sem("lat_T"), {"attn": 2})
        lat_hi = Stage(sem("lat_hi"), {"attn": 4})
        lat_lo = Stage(sem("lat_lo"), {"attn": 4})
        lat_ss = Stage(sem("lat_ss"), {"attn": 1})
        lat_rs = Stage(sem("lat_rs"), {"attn": 1})
        q_done = Stage(sem("q_done"), {"attn": 1})
        kv_done = Stage(sem("kv_done"), {"attn": 1})
        rope_done = Stage(sem("rope_done"), {"attn": 3, "ret": 4})
        qkT_ready = Stage(sem("qkT_ready"), {"attn": MAPS})
        qkT_sb = Stage(sem("qkT_sb"), {"attn": MAPS})
        scores_ready = Stage(sem("scores_ready"), {"attn": MAPS})
        max_ready = Stage(sem("max_ready"), {"attn": MAPS})
        probs_ready = Stage(sem("probs_ready"), {"attn": MAPS})
        pT_ready = Stage(sem("pT_ready"), {"attn": MAPS})
        pT_sb = Stage(sem("pT_sb"), {"attn": MAPS})
        pv_ready = Stage(sem("pv_ready"), {"attn": MAPS})
        head_done = Stage(sem("head_done"), {"attn": MAPS})
        sub_ss = Stage(sem("sub_ss"), {"attn": 1})
        sub_rs = Stage(sem("sub_rs"), {"attn": 1})
        sub_done = Stage(sem("sub_done"), {"attn": 1})
        qk_T = Stage(sem("qk_T"), {"ret": 8})
        qk_a = Stage(sem("qk_a"), {"ret": 4})
        qk_v = Stage(sem("qk_v"), {"ret": 4})
        decay_in = Stage(sem("decay_in"), {"ret": 16})
        ret_scores = Stage(sem("ret_scores"), {"ret": RH})
        ret_decayed = Stage(sem("ret_decayed"), {"ret": RH})
        ret_pv = Stage(sem("ret_pv"), {"ret": RH})
        gn_var = Stage(sem("gn_var"), {"ret": RH, "cf": 1})
        gn_rs = Stage(sem("gn_rs"), {"ret": RH, "cf": 1})
        gn_shift = Stage(sem("gn_shift"), {"ret": RH, "cf": 1})
        y_normed = Stage(sem("y_normed"), {"ret": RH, "cf": 2})
        y_gated = Stage(sem("y_gated"), {"ret": RH})
        sig_ready = Stage(sem("sig_ready"), {"cf": 4})
        glu_done = Stage(sem("glu_done"), {"cf": 4})
        conv_done = Stage(sem("conv_done"), {"cf": 1})
        conv_T = Stage(sem("conv_T"), {"cf": 1})
        silu_done = Stage(sem("silu_done"), {"cf": 4})
        bias_in = Stage(sem("bias_in"), {"cf": 16})
        hh_ready = Stage(sem("hh_ready"), {"cf": 2})
        gates_sb = Stage(sem("gates_sb"), {"sc": 8})
        z_done = Stage(sem("z_done"), {"sc": 4})
        y_ready = Stage(sem("y_ready"), {"sc": 4})
        x_in, ident_in, rope_in, masks_in = sem("x_in"), sem("ident_in"), sem("rope_in"), sem("masks_in")
        rows_in, pos_in, lam_in, inv_in = sem("rows_in"), sem("pos_in"), sem("lam_in"), sem("inv_in")
        rowsT, gains_ready = sem("rowsT"), sem("gains_ready")
        angle_ready, sin_ready, lam_sum, lam_exp = sem("angle_ready"), sem("sin_ready"), sem("lam_sum"), sem("lam_exp")
        halves_ready = sem("halves_ready")
        vec_step, pool_step, act_step = sem("vec_step"), sem("pool_step"), sem("act_step")
        stored = sem("stored")

        sections = [Section(i) for i in range(len(SECTIONS))]

        def gain(name, index, c):
            r = ROWS[name] + index
            return gcol[:, c, r:r + 1]

        def banks(t):
            return ps[:, 2 * t:2 * t + 2, :]

        def two(v):
            return v.rearrange("p (a b) -> p a b", a=2)

        def head(m):
            if m < AH:
                return (pr[:, :, QA + m * AD:QA + (m + 1) * AD], pr[:, :, KA + m * AD:KA + (m + 1) * AD],
                        pr[:, :, VA + m * AD:VA + (m + 1) * AD], AD, AD ** -0.5, 0)
            m -= AH
            if m < BH:
                return qb[:, :, m, :], kb[:, :, m, :], vb[:, :, m, :], BQD, BQD ** -0.5, 1
            m -= BH
            return (pr[:, :, QC0 + m * CQ:QC0 + (m + 1) * CQ], pr[:, :, KC0 + m * CQ:KC0 + (m + 1) * CQ],
                    pr[:, :, VC0 + m // 2 * CV:VC0 + (m // 2 + 1) * CV], CQ, CQ ** -0.5, 1)

        def mixed_head(m):
            c = 64 * (m if m < AH + BH else AH + BH + (m - AH - BH) // 2)
            return mixed[:, :, c:c + 64]

        def row_load(name, src, n=D):
            r = ROWS[name]
            return rows[r:r + src.shape[0], 0:n], src, rows_in

        gn = a["ret_gn_g_2"].rearrange("l (h n) -> (l h) n", n=D)
        row_loads = [row_load("ln1", a["ln1_g"]), row_load("ln2", a["ln2_g"]),
                     row_load("norm", a["norm_g_2"].rearrange("l r n -> (l r) n")), row_load("gn", gn),
                     row_load("bpw1", a["cf_b_pw1_2"].rearrange("l (h n) -> (l h) n", n=D)), row_load("wdw", a["cf_w_dw_2"][0]),
                     row_load("bdw", a["cf_b_dw_2"]), row_load("lng", a["cf_ln_g_2"]), row_load("lnb", a["cf_ln_b_2"]),
                     row_load("wconv", a["sc_w_conv_2"][0]), row_load("qn", a["mla_q_norm_g"], BQ),
                     row_load("kvn", a["mla_kv_norm_g"], BKV)]

        def tiles_of(sec):
            l = sec.layer
            if sec.kind == "attn":
                w = a["w_in"][l].rearrange("(h c p) n -> h p c n", h=2, p=P)
                for g in range(5):
                    n = min(512, IN_COLS - 512 * g)
                    for h in range(2):
                        yield w[h, :, :, 512 * g:512 * g + n]
                yield a["mla_w_uq"][l].rearrange("(c p) n -> p c n", p=P)
                yield a["mla_w_ukv"][l].rearrange("(c p) n -> p c n", p=P)
                yield from down_tiles(a["w_o"][l], D)
            elif sec.kind == "ret":
                w = a["ret_w_in_2"][l // 3].rearrange("(h c p) n -> h p c n", h=2, p=P)
                for g in range(12):
                    for h in range(2):
                        yield w[h, :, :, 512 * g:512 * g + 512]
                yield from down_tiles(a["ret_w_out_2"][l // 3], 2 * D)
            elif sec.kind == "cf":
                w = a["cf_w_pw1_2"][0].rearrange("(c p) n -> p c n", p=P)
                for n in range(8):
                    c = (n % 2) * D + (n // 2) * 256
                    yield w[:, :, c:c + 256]
                yield from down_tiles(a["cf_w_pw2_2"][0], D)
            elif sec.kind == "sc":
                w = a["sc_w_in_2"][0].rearrange("(c p) n -> p c n", p=P)
                outs = list(down_tiles(a["sc_w_out_2"][0], D))
                for n in range(16):
                    if n in SC_OUT:
                        yield outs[SC_OUT.index(n)]
                    else:
                        j = max(i for i in range(4) if SC_UP[i] <= n)
                        c = (n - SC_UP[j]) * D + j * 256
                        yield w[:, :, c:c + 256]

        def down_tiles(w, k):
            for s in range(k // 256):
                yield w[256 * s:256 * s + 256, :].rearrange("(c p) n -> p c n", p=P)

        block = ctx.enter_context(nc.Block())

        @block.sync
        def _(sp):
            def load(sec, c, view, i=0):
                slot, fill = sec.slot(c), sec.fill(c, i)
                sp.wait_ge(lo_ready[slot], fill)
                n = view.shape[1] * view.shape[2]
                dst = w_raw[:, slot, 0:n].rearrange("p (c n) -> p c n", c=view.shape[1])
                sp.dma_start(dst, view).then_inc(raw_in[slot], 16)

            def mlp(sec):
                first = sec.kind == "mlp1"
                up = (a["w_up"] if first else a["mlp_w1_2"])[sec.layer].rearrange("(c p) n -> p c n", p=P)
                down = (a["w_down"] if first else a["mlp_w2_2"])[sec.layer].rearrange("(s c p) n -> s p c n", c=2, p=P)

                def up_tile(k):
                    return up[:, :, bass.ds(k * 256, 256)]

                def down_tile(k):
                    return down[bass.ds(k, 1)].rearrange("a p c n -> p (a c) n")

                load(sec, 0, up_tile(0))
                load(sec, 1, up_tile(1))
                load(sec, 2, down_tile(0))
                with sp.Fori(0, LOOPS) as i:
                    load(sec, 3, up_tile(i * 2 + 2), i)
                    load(sec, 4, down_tile(i * 2 + 1), i)
                    load(sec, 5, up_tile(i * 2 + 3), i)
                    load(sec, 6, down_tile(i * 2 + 2), i)
                load(sec, 27, up_tile(STEPS - 2))
                load(sec, 28, down_tile(STEPS - 3))
                load(sec, 29, up_tile(STEPS - 1))
                load(sec, 30, down_tile(STEPS - 2))
                load(sec, 31, down_tile(STEPS - 1))

            sp.dma_start(x[:], a["x"][0].rearrange("(t p) n -> p t n", p=P)).then_inc(x_in, 16)
            for sec in sections:
                if sec.kind.startswith("mlp"):
                    mlp(sec)
                else:
                    for c, view in enumerate(tiles_of(sec)):
                        load(sec, c, view)
            last = sections[-1]
            sp.wait_ge(x_ready.sem, x_ready.at(last, 2))
            sp.dma_start(out[0].rearrange("(t p) n -> p t n", p=P), x[:]).then_inc(stored, 16)
            sp.wait_ge(stored, 16)

        @block.tensor
        def _(pe):
            def tile_ready(sec, c, i=0):
                slot = sec.slot(c)
                pe.wait_ge(lo_ready[slot], sec.fill(c, i) + 1)
                return slot

            def three(dst, lh, ll, rh, rl, start, stop):
                pe.matmul(dst, lh, rh, start=start, stop=False)
                pe.matmul(dst, lh, rl, start=False, stop=False)
                return pe.matmul(dst, ll, rh, start=False, stop=stop)

            def feed_x(sec):
                pe.wait_ge(x_ready.sem, x_ready.at(sec, 0))
                src = x
                if sec.kind in ("cf", "sc"):
                    pe.wait_ge(xn_ready.sem, xn_ready.at(sec, 1))
                    src = xn
                for b in range(4):
                    for j in range(2):
                        for t in range(NT):
                            c = 2 * b + j
                            ins = pe.transpose(ps[:, 4 + b, j * S + t * P:j * S + (t + 1) * P],
                                               src[:, t, c * P:(c + 1) * P], ident[:])
                    ins.then_inc(xT_ready.sem, 1)

            def wide(sec, g, n, h, bank0):
                slot = tile_ready(sec, 2 * g + h)
                for kl in range(4):
                    kc = 4 * h + kl
                    if g == 0:
                        pe.wait_ge(xT_lo.sem, xT_lo.at(sec, kc + 1))
                    for t in range(NT):
                        wsl = slice(kl * n, kl * n + n)
                        ins = three(ps[:, bank0 + t, 0:n], xT_h[:, kc, t * P:(t + 1) * P], xT_l[:, kc, t * P:(t + 1) * P],
                                    w_hi[:, slot, wsl], w_lo[:, slot, wsl], kc == 0, kc == KC - 1)
                ins.then_inc(used[slot], 1)

            def up(sec, bank, c, i=0, first=False):
                slot = tile_ready(sec, c, i)
                for f in range(2):
                    for kc in range(KC):
                        if first and f == 0:
                            pe.wait_ge(xT_lo.sem, xT_lo.at(sec, max(kc + 1, 2)))
                        wsl = slice(kc * 256 + f * P, kc * 256 + (f + 1) * P)
                        ins = three(ps[:, bank, f * S:(f + 1) * S], w_hi[:, slot, wsl], w_lo[:, slot, wsl],
                                    xT_h[:, kc, :], xT_l[:, kc, :], kc == 0, kc == KC - 1)
                ins.then_inc(used[slot], 1)

            def down(sec, k, us, c, i=0, first=False, last=False):
                pe.wait_ge(feed_lo.sem, feed_lo.at(sec, k + 1))
                slot = tile_ready(sec, c, i)
                for cc in range(2):
                    for t in range(NT):
                        for h in range(2):
                            wsl = slice(cc * D + h * 512, cc * D + h * 512 + 512)
                            ins = three(ps[:, 2 * t + h, :], u_h[:, us, cc, t * P:(t + 1) * P], u_l[:, us, cc, t * P:(t + 1) * P],
                                        w_hi[:, slot, wsl], w_lo[:, slot, wsl], first and cc == 0, last and cc == 1)
                ins.then_inc(used[slot], 1)

            def turn_step(sec, k, src):
                for c in range(2):
                    for t in range(NT):
                        ins = pe.transpose(ps[:, 4 + k % 2, c * S + t * P:c * S + (t + 1) * P],
                                           src[:, t, (2 * k + c) * P:(2 * k + c + 1) * P], ident[:])
                ins.then_inc(feed_T.sem, 1)

            def out_steps(sec, n, tile0, src, ready):
                for k in range(n + 1):
                    if k < n:
                        ready(k)
                        if k >= 2:
                            pe.wait_ge(feed_lo.sem, feed_lo.at(sec, k - 1))
                        turn_step(sec, k, src)
                    if k >= 1:
                        down(sec, k - 1, (k - 1) % 2, tile0 + k - 1, first=k == 1, last=k == n)

            def mlp(sec):
                def up_k(k, par, c, i=0):
                    pe.wait_ge(relu_done.sem, relu_done.at(sec, k - 1))
                    up(sec, 4 + par, c, i)

                feed_x(sec)
                up(sec, 4, 0, first=True)
                up(sec, 5, 1)
                down(sec, 0, 0, 2, first=True)
                with pe.Fori(0, LOOPS) as i:
                    up_k(i * 2 + 2, 0, 3, i)
                    down(sec, i * 2 + 1, 1, 4, i)
                    up_k(i * 2 + 3, 1, 5, i)
                    down(sec, i * 2 + 2, 0, 6, i)
                up_k(STEPS - 2, 0, 27)
                down(sec, STEPS - 3, 1, 28)
                up_k(STEPS - 1, 1, 29)
                down(sec, STEPS - 2, 0, 30)
                down(sec, STEPS - 1, 1, 31, last=True)

            def attn(sec):
                feed_x(sec)
                for g in range(5):
                    if g >= 2:
                        pe.wait_ge(evac_a.sem, evac_a.at(sec, g - 1))
                        pe.wait_ge(evac_v.sem, evac_v.at(sec, g - 1))
                    n = min(512, IN_COLS - 512 * g)
                    wide(sec, g, n, 0, 2 * (g % 2))
                    if g == 4:
                        pe.wait_ge(evac_a.sem, evac_a.at(sec, 4))
                        pe.wait_ge(evac_v.sem, evac_v.at(sec, 4))
                        for b in range(2):
                            for j in range(2):
                                for t in range(NT):
                                    c0 = CQ0 + (2 * b + j) * P
                                    ins = pe.transpose(ps[:, 4 + b, j * S + t * P:j * S + (t + 1) * P],
                                                       pr[:, t, c0:c0 + P], ident[:])
                            ins.then_inc(lat_T.sem, 1)
                    wide(sec, g, n, 1, 2 * (g % 2))
                pe.wait_ge(lat_lo.sem, lat_lo.at(sec, 4))
                pe.wait_ge(evac_a.sem, evac_a.at(sec, 5))
                pe.wait_ge(evac_v.sem, evac_v.at(sec, 5))
                slot = tile_ready(sec, 10)
                n, half = BH * BQD, BH * BQD // 2
                for t in range(NT):
                    for h in range(2):
                        for c in range(BQ // P):
                            wsl = slice(c * n + h * half, c * n + (h + 1) * half)
                            tok = slice(t * P, (t + 1) * P)
                            ins = three(ps[:, 2 * t + h, 0:half], u_h[:, c // 2, c % 2, tok], u_l[:, c // 2, c % 2, tok],
                                        w_hi[:, slot, wsl], w_lo[:, slot, wsl], c == 0, c == BQ // P - 1)
                ins.then_inc(used[slot], 1)
                slot = tile_ready(sec, 11)
                half = BH * (BN + BV) // 2
                for t in range(NT):
                    for h in range(2):
                        wsl = slice(h * half, (h + 1) * half)
                        tok = slice(t * P, (t + 1) * P)
                        ins = three(ps[:, 4 + 2 * t + h, 0:half], u_h[:, 1, 1, tok], u_l[:, 1, 1, tok],
                                    w_hi[:, slot, wsl], w_lo[:, slot, wsl], True, True)
                ins.then_inc(used[slot], 1)
                pe.wait_ge(q_done.sem, q_done.at(sec, 1))
                pe.wait_ge(kv_done.sem, kv_done.at(sec, 1))
                pe.wait_ge(rope_done.sem, rope_done.at(sec, 3))
                for s in range(MAPS + 3):
                    if s < MAPS:
                        m = s
                        q, k, _, d, _, _ = head(m)
                        pe.wait_ge(qkT_sb.sem, qkT_sb.at(sec, m - 1))
                        for j, v in enumerate((q, k)):
                            for t in range(NT):
                                ins = pe.transpose(ps[0:d, 4 + m % 2, j * S + t * P:j * S + (t + 1) * P], v[:, t, :], ident[:])
                        ins.then_inc(qkT_ready.sem, 1)
                    m = s - 1
                    if 0 <= m < MAPS:
                        d = head(m)[3]
                        pe.wait_ge(qkT_sb.sem, qkT_sb.at(sec, m + 1))
                        pe.wait_ge(max_ready.sem, max_ready.at(sec, m - 1))
                        pe.matmul(ps[:, 6 + m % 2, 0:P], qkT[0:d, m % 2, 0:P], qkT[0:d, m % 2, S:S + P], start=True, stop=True)
                        pe.matmul(ps[:, 6 + m % 2, P:P + S], qkT[0:d, m % 2, P:S], qkT[0:d, m % 2, S:2 * S],
                                  start=True, stop=True).then_inc(scores_ready.sem, 1)
                    m = s - 2
                    if 0 <= m < MAPS:
                        pe.wait_ge(probs_ready.sem, probs_ready.at(sec, m + 1))
                        pe.wait_ge(pT_sb.sem, pT_sb.at(sec, m - 1))
                        for j in range(3):
                            ins = pe.transpose(ps[:, m % 2, j * P:(j + 1) * P], sm[:, m % 2, j * P:(j + 1) * P], ident[:])
                        ins.then_inc(pT_ready.sem, 1)
                    m = s - 3
                    if m >= 0:
                        v = head(m)[2]
                        pe.wait_ge(pT_sb.sem, pT_sb.at(sec, m + 1))
                        pe.wait_ge(head_done.sem, head_done.at(sec, m - 1))
                        pe.matmul(ps[:, 2 + m % 2, 0:64], pT[:, m % 2, 0:P], v[:, 0, :], start=True, stop=True)
                        pe.matmul(ps[:, 2 + m % 2, 64:128], pT[:, m % 2, P:2 * P], v[:, 0, :], start=True, stop=False)
                        pe.matmul(ps[:, 2 + m % 2, 64:128], pT[:, m % 2, 2 * P:3 * P], v[:, 1, :], start=False,
                                  stop=True).then_inc(pv_ready.sem, 1)

                def ready(k):
                    pe.wait_ge(head_done.sem, head_done.at(sec, (4, 8, 12, MAPS)[k]))
                    if k == 3:
                        pe.wait_ge(sub_done.sem, sub_done.at(sec, 1))
                pe.wait_ge(head_done.sem, head_done.at(sec, MAPS))
                out_steps(sec, 4, 12, mixed, ready)

            def ret(sec):
                def group(g):
                    if g >= 2:
                        pe.wait_ge(evac_a.sem, evac_a.at(sec, g - 1))
                        pe.wait_ge(evac_v.sem, evac_v.at(sec, min(g - 1, 8)))
                    for h in range(2):
                        wide(sec, g, 512, h, 2 * (g % 2))

                def pv(h):
                    if h >= 2:
                        pe.wait_ge(y_normed.sem, y_normed.at(sec, h - 1))
                    b = 4 + 2 * (h % 2)
                    pe.matmul(ps[:, b, :], rST[:, h, 0:P], rv[:, 0, h * RDV:(h + 1) * RDV], start=True, stop=True)
                    pe.matmul(ps[:, b + 1, :], rST[:, h, P:S], rv[:, 0, h * RDV:(h + 1) * RDV], start=True, stop=False)
                    pe.matmul(ps[:, b + 1, :], rST[:, h, S:S + P], rv[:, 1, h * RDV:(h + 1) * RDV], start=False,
                              stop=True).then_inc(ret_pv.sem, 1)

                feed_x(sec)
                for g in range(8):
                    group(g)
                pe.wait_ge(rope_done.sem, rope_done.at(sec, 4))
                for b in range(8):
                    if b >= 4:
                        pe.wait_ge((qk_a if b % 2 == 0 else qk_v).sem, (qk_a if b % 2 == 0 else qk_v).at(sec, b // 2 - 1))
                    for j in range(2):
                        for t in range(NT):
                            c = 2 * b + j
                            ins = pe.transpose(ps[:, 4 + b % 4, j * S + t * P:j * S + (t + 1) * P],
                                               rqk[:, t, c * P:(c + 1) * P], ident[:])
                    ins.then_inc(qk_T.sem, 1)
                group(8)
                pe.wait_ge(qk_a.sem, qk_a.at(sec, 4))
                pe.wait_ge(qk_v.sem, qk_v.at(sec, 4))
                for h in range(RH):
                    for kt in range(2):
                        for c in range(2):
                            cq, ck = 2 * h + c, 8 + 2 * h + c
                            dst = ps[:, 4 + h, 0:S] if kt == 0 else ps[:, 4 + h, S:S + P]
                            ins = pe.matmul(dst, rqkT[:, ck, kt * P:(kt + 1) * P], rqkT[:, cq, kt * P:S], start=c == 0, stop=c == 1)
                    ins.then_inc(ret_scores.sem, 1)
                group(9)
                pe.wait_ge(evac_v.sem, evac_v.at(sec, 8))
                pe.wait_ge(ret_decayed.sem, ret_decayed.at(sec, RH))
                pv(0)
                pv(1)
                group(10)
                pv(2)
                pv(3)
                group(11)
                pe.wait_ge(evac_a.sem, evac_a.at(sec, 12))
                out_steps(sec, 8, 24, ry, lambda k: pe.wait_ge(y_gated.sem, y_gated.at(sec, RH if k < 2 else k // 2 + 1)))

            def cf(sec):
                feed_x(sec)
                for n in range(8):
                    if n >= 4:
                        pe.wait_ge(glu_done.sem, glu_done.at(sec, n // 2 - 1))
                    up(sec, 4 + n % 4, n, first=n == 0)
                pe.wait_ge(conv_done.sem, conv_done.at(sec, 1))
                pe.wait_ge(glu_done.sem, glu_done.at(sec, 4))
                for c in range(KC):
                    for t in range(NT):
                        ins = pe.transpose(ps[:, 4 + 2 * t + c // 4, (c % 4) * P:(c % 4 + 1) * P], ccv[:, c, t * P:(t + 1) * P], ident[:])
                ins.then_inc(conv_T.sem, 1)
                pe.wait_ge(y_normed.sem, y_normed.at(sec, 2))
                out_steps(sec, 4, 8, ch, lambda k: None)

            def sc(sec):
                feed_x(sec)
                for j in range(4):
                    for q in range(3):
                        m = 3 * j + q
                        if m >= 4:
                            jj, qq = divmod(m - 4, 3)
                            if qq == 2:
                                pe.wait_ge(z_done.sem, z_done.at(sec, jj + 1))
                            else:
                                pe.wait_ge(gates_sb.sem, gates_sb.at(sec, 2 * jj + qq + 1))
                        up(sec, 4 + m % 4, SC_UP[j] + q, first=m == 0)
                    if j >= 1:
                        down(sec, j - 1, (j - 1) % 2, SC_OUT[j - 1], first=j == 1)
                down(sec, 3, 1, SC_OUT[3], last=True)

            pe.wait_ge(ident_in, 16)
            pe.wait_ge(rows_in, 16 * len(row_loads))
            for c in range(KC):
                n = ROWS_AT[c]
                ins = pe.transpose(ps[:, c // 4, (c % 4) * P:(c % 4) * P + n], rows[0:n, c * P:(c + 1) * P], ident[0:n, 0:n])
            ins.then_inc(rowsT, 1)
            pe.wait_ge(x_in, 16)
            pe.wait_ge(gains_ready, 1)
            for sec in sections:
                if sec.kind != "fin":
                    dict(attn=attn, mlp1=mlp, mlp2=mlp, ret=ret, cf=cf, sc=sc)[sec.kind](sec)

        @block.scalar
        def _(act):
            def prepare(sec, c, i=0):
                if sec.tile0 + c + AHEAD >= N_TILES:
                    return
                slot, fill = sec.slot(c + AHEAD), sec.fill(c + AHEAD, i)
                act.wait_ge(raw_in[slot], fill * 16 + 16)
                act.wait_ge(used[slot], fill)
                act.activation(w_hi[:, slot, :], w_raw[:, slot, :], ACT.Copy).then_inc(hi_ready[slot], 1)

            def load_row(sec):
                i = sec.layer
                src = (a["final_g"].rearrange("(a n) -> a n", a=1) if sec.kind == "fin"
                       else a["norm_g_2"][i, 3:4] if sec.kind == "mlp2" else a["norm_g_2"][i, 1:2])
                act.dma_start(row[:], src.to_broadcast([P, D])).then_inc(row_in.sem, 16)

            def start(sec):
                act.wait_ge(x_ready.sem, x_ready.at(sec, 0))
                for t in range(NT):
                    ins = act.activation((junk, tmp)[t], x[:, t, :], ACT.Square, accum_out=ss[:, t:t + 1])
                ins.then_inc(ss_ready.sem, 1)
                if sec.kind not in ("attn", "mlp1"):
                    load_row(sec)

            def feed_x(sec):
                for b in range(4):
                    act.wait_ge(xT_ready.sem, xT_ready.at(sec, b + 1))
                    for j in range(2):
                        c = 2 * b + j
                        name, idx = (("ln1", sec.layer) if sec.kind == "attn" else ("ln2", sec.layer) if sec.kind == "mlp1"
                                     else ("norm", 4 * sec.layer + (2 if sec.kind == "mlp2" else 0)))
                        act.activation(xT_h[:, c, :], ps[:, 4 + b, j * S:(j + 1) * S], ACT.Copy,
                                       scale=gain(name, idx, c)).then_inc(xT_hi.sem, 1)

            def post(sec, last_tile):
                for t in range(NT):
                    act.wait_ge(post_ss.sem, post_ss.at(sec, t))
                    if sec.kind == "cf":
                        act.wait_ge(hh_ready.sem, hh_ready.at(sec, t + 1))
                        src, scale = chh[:, t, :], 1.0
                    else:
                        act.wait_ge(used[sec.slot(last_tile)], sec.fill(last_tile) + 1)
                        src, scale = banks(t), r2[:, t:t + 1] if sec.kind == "mlp2" else 1.0
                    dst = junk if sec.kind == "cf" else two(junk)
                    act.activation(dst, src, ACT.Square, scale=scale, accum_out=pss[:, t:t + 1]).then_inc(post_ss.sem, 1)

            def mlp(sec):
                def square(k, par, c, i=0):
                    act.wait_ge(relu_done.sem, relu_done.at(sec, k + 1))
                    act.wait_ge(feed_lo.sem, feed_lo.at(sec, k - 1))
                    act.activation(sq[:, par, :], relu[:, par, :], ACT.Square).then_inc(sq_done.sem, 1)
                    act.wait_ge(sq_done.sem, sq_done.at(sec, k + 1))

                def high(k, par):
                    act.activation(u_h[:, par, :, :].rearrange("p a b -> p (a b)"), sq[:, par, :], ACT.Copy).then_inc(feed_hi.sem, 1)

                start(sec)
                feed_x(sec)
                prepare(sec, 0)
                square(0, 0, 0)
                high(0, 0)
                prepare(sec, 1)
                square(1, 1, 1)
                high(1, 1)
                prepare(sec, 2)
                with act.Fori(0, LOOPS) as i:
                    for par in range(2):
                        prepare(sec, 3 + 2 * par, i)
                        square(i * 2 + 2 + par, par, None)
                        act.wait_ge(used[sec.slot(2 if par == 0 else 4)], sec.fill(2 if par == 0 else 4, i) + 1)
                        high(i * 2 + 2 + par, par)
                        prepare(sec, 4 + 2 * par, i)
                for par in range(2):
                    prepare(sec, 27 + 2 * par)
                    square(STEPS - 2 + par, par, None)
                    act.wait_ge(used[sec.slot(26 + 2 * par)], sec.fill(26 + 2 * par) + 1)
                    high(STEPS - 2 + par, par)
                    prepare(sec, 28 + 2 * par)
                prepare(sec, 31)
                if sec.kind == "mlp2":
                    post(sec, 31)

            def evac(sec, g, n):
                act.wait_ge(used[sec.slot(2 * g + 1)], sec.fill(2 * g + 1) + 1)
                b = 2 * (g % 2)
                if sec.kind == "attn":
                    ins = act.activation(pr[:, 0, 512 * g:512 * g + n], ps[:, b, 0:n], ACT.Copy, scale=rstd[:, 0:1])
                elif g < 8:
                    dst = rqk[:, 0, 512 * g:512 * g + 512] if g < 4 else rv[:, 0, 512 * (g - 4):512 * (g - 3)]
                    ins = act.activation(dst, ps[:, b, :], ACT.Copy, scale=rstd[:, 0:1])
                else:
                    for t in range(NT):
                        ins = act.activation(rg[:, t, 512 * (g - 8):512 * (g - 7)], ps[:, b + t, :], ACT.Silu, scale=rstd[:, t:t + 1])
                ins.then_inc(evac_a.sem, 1)

            def attn(sec):
                start(sec)
                feed_x(sec)
                act.wait_ge(rstd_ready.sem, rstd_ready.at(sec, 1))
                for g in range(5):
                    prepare(sec, 2 * g)
                    if g > 0:
                        evac(sec, g - 1, 512)
                    if g == 4:
                        for c in range(4):
                            act.wait_ge(lat_T.sem, lat_T.at(sec, c // 2 + 1))
                            name = "qn" if c < 3 else "kvn"
                            act.activation(u_h[:, c // 2, c % 2, :], ps[:, 4 + c // 2, (c % 2) * S:(c % 2 + 1) * S], ACT.Copy,
                                           scale=gain(name, sec.layer, c % 3)).then_inc(lat_hi.sem, 1)
                        act.wait_ge(evac_v.sem, evac_v.at(sec, 4))
                        for j, (c0, n) in enumerate(((CQ0, BQ), (CKV0, BKV))):
                            for t in range(NT):
                                ins = act.activation(junk[:, j * 768 + t * n:j * 768 + (t + 1) * n], pr[:, t, c0:c0 + n], ACT.Square,
                                                     accum_out=lss[:, 2 * j + t:2 * j + t + 1])
                        ins.then_inc(lat_ss.sem, 1)
                    prepare(sec, 2 * g + 1)
                prepare(sec, 10)
                evac(sec, 4, IN_COLS - 2048)
                prepare(sec, 11)
                act.wait_ge(used[sec.slot(10)], sec.fill(10) + 1)
                act.wait_ge(lat_rs.sem, lat_rs.at(sec, 1))
                for t in range(NT):
                    for h in range(2):
                        n = BH * BQD // 2
                        ins = act.activation(qb[:, t, :, :].rearrange("p h d -> p (h d)")[:, h * n:(h + 1) * n],
                                             ps[:, 2 * t + h, 0:n], ACT.Copy, scale=lrs[:, t:t + 1])
                ins.then_inc(q_done.sem, 1)
                prepare(sec, 12)
                for s in range(MAPS + 2):
                    m = s - 1
                    if 0 <= m < MAPS:
                        scale = head(m)[4]
                        act.wait_ge(max_ready.sem, max_ready.at(sec, m + 1))
                        for t in range(NT):
                            c = slice(0, P) if t == 0 else slice(P, P + S)
                            j = 2 * (m % 2) + t
                            ins = act.activation(sm[:, m % 2, c], sm[:, m % 2, c], ACT.Exp, bias=negmax[:, j:j + 1], scale=-1.0,
                                                 accum_out=zsum[:, j:j + 1])
                        ins.then_inc(probs_ready.sem, 1)
                    if s < MAPS:
                        m = s
                        act.wait_ge(qkT_ready.sem, qkT_ready.at(sec, m + 1))
                        act.wait_ge(scores_ready.sem, scores_ready.at(sec, m - 1))
                        d = head(m)[3]
                        act.activation(qkT[0:d, m % 2, :], ps[0:d, 4 + m % 2, :], ACT.Copy).then_inc(qkT_sb.sem, 1)
                for k in range(4):
                    act.wait_ge(feed_T.sem, feed_T.at(sec, k + 1))
                    if k >= 2:
                        act.wait_ge(used[sec.slot(12 + k - 2)], sec.fill(12 + k - 2) + 1)
                    act.activation(u_h[:, k % 2, :, :].rearrange("p a b -> p (a b)"), ps[:, 4 + k % 2, :], ACT.Copy).then_inc(feed_hi.sem, 1)
                    if k >= 1:
                        prepare(sec, 12 + k)

            def ret(sec):
                def norm(h):
                    act.wait_ge(gn_shift.sem, gn_shift.at(sec, h + 1))
                    for t in range(NT):
                        j = 2 * h + t
                        ins = act.activation(ry[:, t, h * RDV:(h + 1) * RDV], ps[:, 4 + 2 * (h % 2) + t, :], ACT.Identity,
                                             scale=grs[:, j:j + 1], bias=gshift[:, j:j + 1])
                    ins.then_inc(y_normed.sem, 1)

                start(sec)
                feed_x(sec)
                act.wait_ge(rstd_ready.sem, rstd_ready.at(sec, 1))
                for g in range(8):
                    prepare(sec, 2 * g)
                    if g > 0:
                        evac(sec, g - 1, 512)
                    prepare(sec, 2 * g + 1)
                prepare(sec, 16)
                evac(sec, 7, 512)
                for b in range(0, 8, 2):
                    act.wait_ge(qk_T.sem, qk_T.at(sec, b + 1))
                    act.activation(rqkT[:, 2 * b:2 * b + 2, :].rearrange("p a b -> p (a b)"), ps[:, 4 + b % 4, :],
                                   ACT.Copy).then_inc(qk_a.sem, 1)
                act.wait_ge(qk_T.sem, qk_T.at(sec, 8))
                act.dma_start(rD.rearrange("p h n -> p (h n)"), a["c_decay"]).then_inc(decay_in.sem, 16)
                prepare(sec, 17)
                prepare(sec, 18)
                evac(sec, 8, 512)
                prepare(sec, 19)
                prepare(sec, 20)
                evac(sec, 9, 512)
                norm(0)
                norm(1)
                prepare(sec, 21)
                prepare(sec, 22)
                evac(sec, 10, 512)
                norm(2)
                norm(3)
                prepare(sec, 23)
                prepare(sec, 24)
                evac(sec, 11, 512)
                for k in range(8):
                    act.wait_ge(feed_T.sem, feed_T.at(sec, k + 1))
                    if k >= 2:
                        act.wait_ge(used[sec.slot(24 + k - 2)], sec.fill(24 + k - 2) + 1)
                    for c in range(2):
                        g = 2 * (sec.layer // 3) + (2 * k + c) // 8
                        ins = act.activation(u_h[:, k % 2, c, :], ps[:, 4 + k % 2, c * S:(c + 1) * S], ACT.Copy,
                                             scale=gain("gn", g, (2 * k + c) % 8))
                    ins.then_inc(feed_hi.sem, 1)
                    if k >= 1:
                        prepare(sec, 24 + k)
                post(sec, 31)

            def cf(sec):
                start(sec)
                act.dma_start(cbias, a["cf_b_pw2_2"].to_broadcast([P, D])).then_inc(bias_in.sem, 16)
                feed_x(sec)
                for j in range(4):
                    prepare(sec, 2 * j)
                    prepare(sec, 2 * j + 1)
                    act.wait_ge(used[sec.slot(2 * j + 1)], sec.fill(2 * j + 1) + 1)
                    act.wait_ge(glu_done.sem, glu_done.at(sec, j - 1))
                    for f in range(2):
                        c = 2 * j + f
                        ins = act.activation(csg[:, j % 2, f, :], ps[:, 4 + (2 * j + 1) % 4, f * S:(f + 1) * S], ACT.Sigmoid,
                                             bias=gain("bpw1", 1, c))
                    ins.then_inc(sig_ready.sem, 1)
                prepare(sec, 8)
                act.wait_ge(gn_shift.sem, gn_shift.at(sec, 1))
                for t in range(NT):
                    act.activation(two(ch[:, t, :]), ps[:, 4 + 2 * t:6 + 2 * t, :], ACT.Identity, scale=grs[:, t:t + 1],
                                   bias=gshift[:, t:t + 1]).then_inc(y_normed.sem, 1)
                for k in range(4):
                    act.wait_ge(feed_T.sem, feed_T.at(sec, k + 1))
                    act.wait_ge(feed_lo.sem, feed_lo.at(sec, k - 1))
                    for f in range(2):
                        c = 2 * k + f
                        ins = act.activation(csl[:, k % 2, f, :], ps[:, 4 + k % 2, f * S:(f + 1) * S], ACT.Silu,
                                             scale=gain("lng", 0, c), bias=gain("lnb", 0, c))
                    ins.then_inc(silu_done.sem, 1)
                    act.wait_ge(silu_done.sem, silu_done.at(sec, k + 1))
                    if k >= 2:
                        act.wait_ge(used[sec.slot(8 + k - 2)], sec.fill(8 + k - 2) + 1)
                    act.activation(u_h[:, k % 2, :, :], csl[:, k % 2, :, :], ACT.Copy).then_inc(feed_hi.sem, 1)
                    if k >= 1:
                        prepare(sec, 8 + k)
                post(sec, 11)

            def sc(sec):
                def high(k):
                    act.wait_ge(y_ready.sem, y_ready.at(sec, k + 1))
                    if k >= 2:
                        act.wait_ge(used[sec.slot(SC_OUT[k - 2])], sec.fill(SC_OUT[k - 2]) + 1)
                    act.activation(u_h[:, k % 2, :, :], sy[:, k % 2, :, :], ACT.Copy).then_inc(feed_hi.sem, 1)

                start(sec)
                feed_x(sec)
                for n in range(16):
                    prepare(sec, n)
                    if n in SC_OUT:
                        continue
                    j = max(i for i in range(4) if SC_UP[i] <= n)
                    q = n - SC_UP[j]
                    if q < 2:
                        act.wait_ge(used[sec.slot(n)], sec.fill(n) + 1)
                        act.wait_ge(y_ready.sem, y_ready.at(sec, j - 1))
                        act.wait_ge(z_done.sem, z_done.at(sec, j - 1))
                        dst = (sgb, sgc)[q]
                        act.activation(dst[:, j % 2, :, :].rearrange("p a b -> p (a b)"), ps[:, 4 + (3 * j + q) % 4, :],
                                       ACT.Copy).then_inc(gates_sb.sem, 1)
                    if q == 0 and j > 0:
                        high(j - 1)
                    if n == SC_UP[3] + 2:
                        high(3)
                post(sec, 15)

            for dst, src, s in ((ident[:], a["c_ident"], ident_in), *row_loads,
                                (rope[:], a["c_rope"], rope_in), (masks[:], a["c_masks"], masks_in),
                                (pos_i[:], a["positions_2"][0].rearrange("(t p) -> p t", p=P), pos_in),
                                (s_inv, a["c_invfreq"].to_broadcast([P, 128]), inv_in),
                                (lam_rows[:].rearrange("p l n -> p (l n)"), a["diff_lambda"].rearrange("(o l) a b -> o (l a b)", o=1).to_broadcast([P, DEPTH1 * 4 * CQ]), lam_in),
                                (sub_g[:].rearrange("p l n -> p (l n)"), a["diff_subln_g"].rearrange("(o l) n -> o (l n)", o=1).to_broadcast([P, DEPTH1 * CV]), lam_in)):
                with nc.allow_non_contiguous_dma(reason="256 positions"):
                    act.dma_start(dst, src).then_inc(s, 16)
            act.wait_ge(angle_ready, 1)
            act.activation(cs[:, :, 1, :], s_r, ACT.Sin)
            act.activation(s_n, s_r, ACT.Sin, scale=0.5).then_inc(sin_ready, 1)
            act.wait_ge(lam_sum, 1)
            act.activation(lexp, lam4, ACT.Exp).then_inc(lam_exp, 1)
            for c in range(AHEAD):
                prepare(sections[0], c - AHEAD)
            act.wait_ge(x_in, 16)
            act.wait_ge(gains_ready, 1)
            for sec in sections:
                dict(attn=attn, mlp1=mlp, mlp2=mlp, ret=ret, cf=cf, sc=sc, fin=start)[sec.kind](sec)

        @block.gpsimd
        def _(pool):
            step = Chain(pool, pool_step)

            def prepare(sec, c, i=0):
                t = sec.tile0 + c + AHEAD
                if t < N_TILES and owner(t) == "gpsimd":
                    slot = sec.slot(c + AHEAD)
                    pool.wait_ge(hi_ready[slot], sec.fill(c + AHEAD, i) + 1)
                    pool.tensor_tensor(w_lo[:, slot, :], w_raw[:, slot, :], w_hi[:, slot, :].bitcast(F32),
                                       ALU.subtract).then_inc(lo_ready[slot], 1)

            def rsqrt(dst, mid, src, n, scale, eps):
                step.link(pool.tensor_scalar(mid, src, scale, eps, ALU.mult, ALU.add))
                return pool.tensor_tensor(dst, mid, mhalf[:, 0:n], ALU.pow)

            def start(sec):
                pool.wait_ge(ss_ready.sem, ss_ready.at(sec, 1))
                rsqrt(rstd, ms, ss, 2, 1.0 / D, EPS).then_inc(rstd_ready.sem, 1)

            def post(sec):
                for t in range(NT):
                    pool.wait_ge(post_ss.sem, post_ss.at(sec, t + 1))
                    rsqrt(prs[:, t:t + 1], pms[:, t:t + 1], pss[:, t:t + 1], 1, 1.0 / D, EPS).then_inc(post_rs.sem, 1)

            def mlp(sec):
                start(sec)
                for c in range(3):
                    prepare(sec, c)
                with pool.Fori(0, LOOPS) as i:
                    for c in range(3, 7):
                        prepare(sec, c, i)
                for c in range(27, 32):
                    prepare(sec, c)
                if sec.kind == "mlp2":
                    post(sec)

            def attn(sec):
                start(sec)
                for c in range(9):
                    prepare(sec, c)
                pool.wait_ge(lat_ss.sem, lat_ss.at(sec, 1))
                step.link(pool.tensor_scalar(lms[:, 0:2], lss[:, 0:2], 1.0 / BQ, EPS, ALU.mult, ALU.add))
                step.link(pool.tensor_scalar(lms[:, 2:4], lss[:, 2:4], 1.0 / BKV, EPS, ALU.mult, ALU.add))
                pool.tensor_tensor(lrs, lms, mhalf[:, 0:4], ALU.pow).then_inc(lat_rs.sem, 1)
                for c in range(9, 13):
                    prepare(sec, c)
                pool.wait_ge(sub_ss.sem, sub_ss.at(sec, 1))
                rsqrt(srs, sms, sss, 8, 1.0 / CV, SUB_EPS).then_inc(sub_rs.sem, 1)
                for c in range(13, 16):
                    prepare(sec, c)

            def ret(sec):
                def var(h):
                    pool.wait_ge(gn_var.sem, gn_var.at(sec, h + 1))
                    j = 2 * h
                    rsqrt(grs[:, j:j + 2], gvar[:, j:j + 2], mv[:, j:j + 2, 1], 2, 1.0, LN_EPS).then_inc(gn_rs.sem, 1)

                start(sec)
                for c in range(21):
                    prepare(sec, c)
                var(0)
                var(1)
                for c in range(21, 23):
                    prepare(sec, c)
                var(2)
                var(3)
                for c in range(23, 32):
                    prepare(sec, c)
                post(sec)

            def cf(sec):
                start(sec)
                for c in range(9):
                    prepare(sec, c)
                pool.wait_ge(gn_var.sem, gn_var.at(sec, 1))
                rsqrt(grs[:, 0:2], gvar[:, 0:2], mv[:, 0:2, 1], 2, 1.0, LN_EPS).then_inc(gn_rs.sem, 1)
                for c in range(9, 12):
                    prepare(sec, c)
                post(sec)

            def sc(sec):
                start(sec)
                for c in range(16):
                    prepare(sec, c)
                post(sec)

            step.link(pool.memset(mhalf[:], -0.5))
            for c in range(AHEAD):
                prepare(sections[0], c - AHEAD)
            for sec in sections:
                dict(attn=attn, mlp1=mlp, mlp2=mlp, ret=ret, cf=cf, sc=sc, fin=start)[sec.kind](sec)

        @block.vector
        def _(vec):
            step = Chain(vec, vec_step)
            tt, ts, stt = vec.tensor_tensor, vec.tensor_scalar, vec.scalar_tensor_tensor

            def prepare(sec, c, i=0):
                t = sec.tile0 + c + AHEAD
                if t < N_TILES and owner(t) == "vector":
                    slot = sec.slot(c + AHEAD)
                    vec.wait_ge(hi_ready[slot], sec.fill(c + AHEAD, i) + 1)
                    vec.tensor_tensor(w_lo[:, slot, :], w_raw[:, slot, :], w_hi[:, slot, :].bitcast(F32),
                                       ALU.subtract).then_inc(lo_ready[slot], 1)

            def feed_x(sec):
                name, idx = (("ln1", sec.layer) if sec.kind == "attn" else ("ln2", sec.layer) if sec.kind == "mlp1"
                             else ("norm", 4 * sec.layer + (2 if sec.kind == "mlp2" else 0)))
                for c in range(KC):
                    vec.wait_ge(xT_hi.sem, xT_hi.at(sec, c // 2 * 2 + 2))
                    stt(xT_l[:, c, :], ps[:, 4 + c // 2, (c % 2) * S:(c % 2 + 1) * S], gain(name, idx, c),
                        xT_h[:, c, :].bitcast(F32), ALU.mult, ALU.subtract).then_inc(xT_lo.sem, 1)

            def normalise(sec):
                vec.wait_ge(rstd_ready.sem, rstd_ready.at(sec, 1))
                for t in range(NT):
                    ins = ts(xn[:, t, :], x[:, t, :], rstd[:, t:t + 1], None, ALU.mult)
                ins.then_inc(xn_ready.sem, 1)

            def post(sec):
                vec.wait_ge(row_in.sem, row_in.at(sec, 16))
                for t in range(NT):
                    vec.wait_ge(post_rs.sem, post_rs.at(sec, t + 1))
                    f = prs[:, t:t + 1]
                    if sec.kind == "mlp2":
                        step.link(tt(coef[:, t:t + 1], prs[:, t:t + 1], r2[:, t:t + 1], ALU.mult))
                        f = coef[:, t:t + 1]
                    if sec.kind == "cf":
                        ins = stt(tmp, chh[:, t, :], f, row[:], ALU.mult, ALU.mult)
                    else:
                        ins = stt(two(tmp), banks(t), f, two(row[:]), ALU.mult, ALU.mult)
                    step.link(ins)
                    tt(x[:, t, :], x[:, t, :], tmp, ALU.add).then_inc(x_ready.sem, 1)
                    vec.wait_ge(x_ready.sem, x_ready.at(sec, t + 1))

            def mlp(sec):
                def rectify(k, par, c, i=0):
                    vec.wait_ge(used[sec.slot(c)], sec.fill(c, i) + 1)
                    vec.wait_ge(sq_done.sem, sq_done.at(sec, k - 1))
                    ts(relu[:, par, :], ps[:, 4 + par, :], 0.0, None, ALU.max).then_inc(relu_done.sem, 1)

                def low(k, par):
                    vec.wait_ge(feed_hi.sem, feed_hi.at(sec, k + 1))
                    tt(u_l[:, par, :, :].rearrange("p a b -> p (a b)"), sq[:, par, :],
                       u_h[:, par, :, :].rearrange("p a b -> p (a b)").bitcast(F32), ALU.subtract).then_inc(feed_lo.sem, 1)

                feed_x(sec)
                vec.wait_ge(rstd_ready.sem, rstd_ready.at(sec, 1))
                step.link(vec.reciprocal(r2, ms))
                prepare(sec, 0)
                rectify(0, 0, 0)
                low(0, 0)
                prepare(sec, 1)
                rectify(1, 1, 1)
                low(1, 1)
                prepare(sec, 2)
                with vec.Fori(0, LOOPS) as i:
                    for par in range(2):
                        prepare(sec, 3 + 2 * par, i)
                        rectify(i * 2 + 2 + par, par, 3 + 2 * par, i)
                        low(i * 2 + 2 + par, par)
                        prepare(sec, 4 + 2 * par, i)
                for par in range(2):
                    prepare(sec, 27 + 2 * par)
                    rectify(STEPS - 2 + par, par, 27 + 2 * par)
                    low(STEPS - 2 + par, par)
                    prepare(sec, 28 + 2 * par)
                prepare(sec, 31)
                if sec.kind == "mlp2":
                    post(sec)
                else:
                    vec.wait_ge(used[sec.slot(31)], sec.fill(31) + 1)
                    for t in range(NT):
                        stt(two(x[:, t, :]), banks(t), r2[:, t:t + 1], two(x[:, t, :]), ALU.mult,
                            ALU.add).then_inc(x_ready.sem, 1)
                    vec.wait_ge(x_ready.sem, x_ready.at(sec, 2))

            def rotate(v, h, half, cos, sin, ra, rb):
                shape = [P, h, 2, half]
                v4 = v.rearrange("p h (a d) -> p h a d", a=2)
                ra4 = ra.rearrange("p (h a d) -> p h a d", h=h, a=2)
                rb4 = rb.rearrange("p (h a d) -> p h a d", h=h, a=2)
                tt(ra4, v4, cos.unsqueeze(1).unsqueeze(1).to_broadcast(shape), ALU.mult)
                step.link(tt(rb4, v4, sin.unsqueeze(1).unsqueeze(1).to_broadcast(shape), ALU.mult))
                tt(v4[:, :, 0, :], ra4[:, :, 0, :], rb4[:, :, 1, :], ALU.subtract)
                return tt(v4[:, :, 1, :], rb4[:, :, 0, :], ra4[:, :, 1, :], ALU.add)

            def attn(sec):
                c64, s64 = [rope[:, t, 0:32] for t in range(NT)], [rope[:, t, 32:64] for t in range(NT)]
                c32, s32 = [rope[:, t, 64:80] for t in range(NT)], [rope[:, t, 80:96] for t in range(NT)]

                def evac(g, n):
                    vec.wait_ge(used[sec.slot(2 * g + 1)], sec.fill(2 * g + 1) + 1)
                    ts(pr[:, 1, 512 * g:512 * g + n], ps[:, 2 * (g % 2) + 1, 0:n], rstd[:, 1:2], None,
                       ALU.mult).then_inc(evac_v.sem, 1)

                feed_x(sec)
                vec.wait_ge(rstd_ready.sem, rstd_ready.at(sec, 1))
                for g in range(4):
                    prepare(sec, 2 * g)
                    prepare(sec, 2 * g + 1)
                    evac(g, 512)
                    if g == 1:
                        vec.wait_ge(evac_a.sem, evac_a.at(sec, 2))
                        vec.wait_ge(evac_v.sem, evac_v.at(sec, 2))
                        for t in range(NT):
                            ins = rotate(pr[:, t, QA:VA].rearrange("p (h d) -> p h d", d=AD), 2 * AH, AD // 2, c64[t], s64[t], rope_a, rope_b)
                            step.link(ins) if t == 0 else ins.then_inc(rope_done.sem, 1)
                prepare(sec, 8)
                for c in range(4):
                    vec.wait_ge(lat_hi.sem, lat_hi.at(sec, c // 2 * 2 + 2))
                    stt(u_l[:, c // 2, c % 2, :], ps[:, 4 + c // 2, (c % 2) * S:(c % 2 + 1) * S],
                        gain("qn" if c < 3 else "kvn", sec.layer, c % 3), u_h[:, c // 2, c % 2, :].bitcast(F32),
                        ALU.mult, ALU.subtract).then_inc(lat_lo.sem, 1)
                prepare(sec, 9)
                prepare(sec, 10)
                evac(4, IN_COLS - 2048)
                vec.wait_ge(evac_a.sem, evac_a.at(sec, 5))
                vec.wait_ge(evac_v.sem, evac_v.at(sec, 5))
                vec.wait_ge(rope_done.sem, rope_done.at(sec, 1))
                for t in range(NT):
                    step.link(rotate(pr[:, t, KR0:KR0 + BR].unsqueeze(1), 1, BR // 2, c32[t], s32[t], rope_a[:, 0:BR], rope_b[:, 0:BR]))
                    ins = rotate(pr[:, t, QC0:VC0].rearrange("p (h d) -> p h d", d=CQ), 4 * CH, CQ // 2, c32[t], s32[t],
                                 rope_a[:, 0:512], rope_b[:, 0:512])
                    step.link(ins) if t == 0 else ins.then_inc(rope_done.sem, 1)
                vec.wait_ge(rope_done.sem, rope_done.at(sec, 2))
                prepare(sec, 11)
                vec.wait_ge(used[sec.slot(11)], sec.fill(11) + 1)
                vec.wait_ge(lat_rs.sem, lat_rs.at(sec, 1))
                for t in range(NT):
                    for h in range(2):
                        kv = ps[:, 4 + 2 * t + h, 0:384].rearrange("p (h d) -> p h d", h=3)
                        ts(kb[:, t, 3 * h:3 * h + 3, 0:BN], kv[:, :, 0:BN], lrs[:, 2 + t:3 + t], None, ALU.mult)
                        ts(vb[:, t, 3 * h:3 * h + 3, :], kv[:, :, BN:BN + BV], lrs[:, 2 + t:3 + t], None, ALU.mult)
                    ins = vec.tensor_copy(kb[:, t, :, BN:BQD], pr[:, t, KR0:KR0 + BR].unsqueeze(1).to_broadcast([P, BH, BR]))
                ins.then_inc(kv_done.sem, 1)
                vec.wait_ge(q_done.sem, q_done.at(sec, 1))
                for t in range(NT):
                    ins = rotate(qb[:, t, :, BN:BQD], BH, BR // 2, c32[t], s32[t], rope_a[:, 0:BH * BR], rope_b[:, 0:BH * BR])
                    step.link(ins) if t == 0 else ins.then_inc(rope_done.sem, 1)
                prepare(sec, 12)
                for s in range(1, MAPS + 3):
                    m = s - 1
                    if m < MAPS:
                        scale = head(m)[4]
                        mask = masks[:, head(m)[5], :]
                        vec.wait_ge(scores_ready.sem, scores_ready.at(sec, m + 1))
                        vec.wait_ge(pT_ready.sem, pT_ready.at(sec, m - 1))
                        for t in range(NT):
                            c = slice(0, P) if t == 0 else slice(P, P + S)
                            j = 2 * (m % 2) + t
                            ins = vec.tensor_tensor_reduce(sm[:, m % 2, c], ps[:, 6 + m % 2, c], mask[:, c], -scale, 3.0e38,
                                                           ALU.add, ALU.min, negmax[:, j:j + 1])
                        ins.then_inc(max_ready.sem, 1)
                    m = s - 3
                    if m >= 0:
                        vec.wait_ge(pv_ready.sem, pv_ready.at(sec, m + 1))
                        dst = mixed_head(m)
                        j = 2 * (m % 2)
                        rzb = rz[:, j:j + 2].unsqueeze(2).to_broadcast([P, NT, 64])
                        src = ps[:, 2 + m % 2, 0:128].rearrange("p (t d) -> p t d", t=NT)
                        second = m >= AH + BH and (m - AH - BH) % 2 == 1
                        if not second:
                            tt(dst, src, rzb, ALU.mult).then_inc(head_done.sem, 1)
                        else:
                            t2 = tmp[:, 0:128].rearrange("p (t d) -> p t d", t=NT)
                            step.link(tt(t2, src, rzb, ALU.mult))
                            stt(dst, t2, neglam[:, sec.layer:sec.layer + 1], dst, ALU.mult, ALU.add).then_inc(head_done.sem, 1)
                            vec.wait_ge(head_done.sem, head_done.at(sec, m + 1))
                    m = s - 2
                    if 0 <= m < MAPS:
                        vec.wait_ge(pT_ready.sem, pT_ready.at(sec, m + 1))
                        vec.wait_ge(pv_ready.sem, pv_ready.at(sec, m - 1))
                        vec.tensor_copy(pT[:, m % 2, :], ps[:, m % 2, 0:384]).then_inc(pT_sb.sem, 1)
                        j = 2 * (m % 2)
                        step.link(vec.reciprocal(rz[:, j:j + 2], zsum[:, j:j + 2]))
                vec.wait_ge(head_done.sem, head_done.at(sec, MAPS))
                mc = mixed[:, :, D - CH * CV:D]
                t2 = tmp[:, 0:512].rearrange("p (t n) -> p t n", t=NT)
                step.link(tt(t2, mc, mc, ALU.mult))
                vec.tensor_reduce(sss, tmp[:, 0:512].rearrange("p (h d) -> p h d", d=CV), AX.X, ALU.add).then_inc(sub_ss.sem, 1)
                vec.wait_ge(sub_rs.sem, sub_rs.at(sec, 1))
                for t in range(NT):
                    v = mc[:, t, :].rearrange("p (h d) -> p h d", d=CV)
                    step.link(tt(v, v, srs[:, 4 * t:4 * t + 4].unsqueeze(2).to_broadcast([P, CH, CV]), ALU.mult))
                    ins = tt(v, v, sub_g[:, sec.layer, :].unsqueeze(1).to_broadcast([P, CH, CV]), ALU.mult)
                ins.then_inc(sub_done.sem, 1)
                for k in range(4):
                    vec.wait_ge(feed_hi.sem, feed_hi.at(sec, k + 1))
                    tt(u_l[:, k % 2, :, :].rearrange("p a b -> p (a b)"), ps[:, 4 + k % 2, :],
                       u_h[:, k % 2, :, :].rearrange("p a b -> p (a b)").bitcast(F32), ALU.subtract).then_inc(feed_lo.sem, 1)
                    if k >= 1:
                        prepare(sec, 12 + k)
                vec.wait_ge(used[sec.slot(15)], sec.fill(15) + 1)
                for t in range(NT):
                    tt(two(x[:, t, :]), banks(t), two(x[:, t, :]), ALU.add).then_inc(x_ready.sem, 1)
                vec.wait_ge(x_ready.sem, x_ready.at(sec, 2))

            def ret(sec):
                def evac(g):
                    vec.wait_ge(used[sec.slot(2 * g + 1)], sec.fill(2 * g + 1) + 1)
                    dst = rqk[:, 1, 512 * g:512 * g + 512] if g < 4 else rv[:, 1, 512 * (g - 4):512 * (g - 3)]
                    ts(dst, ps[:, 2 * (g % 2) + 1, :], rstd[:, 1:2], None, ALU.mult).then_inc(evac_v.sem, 1)

                def statistics(h):
                    vec.wait_ge(ret_pv.sem, ret_pv.at(sec, h + 1))
                    for t in range(NT):
                        ins = vec.bn_stats(bns[:, t, :], ps[:, 4 + 2 * (h % 2) + t, :])
                    step.link(ins)
                    for t in range(NT):
                        ins = vec.bn_aggr(mv[:, 2 * h + t, :], bns[:, t, :])
                    ins.then_inc(gn_var.sem, 1)
                    vec.wait_ge(gn_rs.sem, gn_rs.at(sec, h + 1))
                    j = 2 * h
                    stt(gshift[:, j:j + 2], mv[:, j:j + 2, 0], -1.0, grs[:, j:j + 2], ALU.mult, ALU.mult).then_inc(gn_shift.sem, 1)

                def gate(h):
                    vec.wait_ge(y_normed.sem, y_normed.at(sec, h + 1))
                    vec.wait_ge(evac_a.sem, evac_a.at(sec, 8 + h + 1))
                    v = ry[:, :, h * RDV:(h + 1) * RDV]
                    tt(v, v, rg[:, :, h * RDV:(h + 1) * RDV], ALU.mult).then_inc(y_gated.sem, 1)

                feed_x(sec)
                vec.wait_ge(rstd_ready.sem, rstd_ready.at(sec, 1))
                n = 0
                for g in range(8):
                    evac(g)
                    if g in (3, 4, 5, 6):
                        t, j = divmod(g - 3, 2)
                        vec.wait_ge(evac_a.sem, evac_a.at(sec, 4))
                        if g == 3:
                            vec.wait_ge(evac_v.sem, evac_v.at(sec, 4))
                        i = (g - 3) % 2
                        ins = rotate(rqk[:, t, j * D:(j + 1) * D].rearrange("p (h d) -> p h d", d=RDK), RH, RDK // 2,
                                     cs[:, t, 0, :], cs[:, t, 1, :], rope_ra[i].rearrange("p a b -> p (a b)"),
                                     rope_rb[i].rearrange("p a b -> p (a b)"))
                        ins.then_inc(rope_done.sem, 1)
                        vec.wait_ge(rope_done.sem, rope_done.at(sec, g - 2))
                for b in range(1, 8, 2):
                    vec.wait_ge(qk_T.sem, qk_T.at(sec, b + 1))
                    vec.tensor_copy(rqkT[:, 2 * b:2 * b + 2, :].rearrange("p a b -> p (a b)"), ps[:, 4 + b % 4, :]).then_inc(qk_v.sem, 1)
                vec.wait_ge(decay_in.sem, decay_in.at(sec, 16))
                for h in range(RH):
                    vec.wait_ge(ret_scores.sem, ret_scores.at(sec, h + 1))
                    tt(rST[:, h, :], ps[:, 4 + h, 0:384], rD[:, h, :], ALU.mult).then_inc(ret_decayed.sem, 1)
                statistics(0)
                statistics(1)
                gate(0)
                gate(1)
                statistics(2)
                statistics(3)
                gate(2)
                gate(3)
                for k in range(8):
                    vec.wait_ge(feed_hi.sem, feed_hi.at(sec, k + 1))
                    for c in range(2):
                        g = 2 * (sec.layer // 3) + (2 * k + c) // 8
                        ins = stt(u_l[:, k % 2, c, :], ps[:, 4 + k % 2, c * S:(c + 1) * S], gain("gn", g, (2 * k + c) % 8),
                                  u_h[:, k % 2, c, :].bitcast(F32), ALU.mult, ALU.subtract)
                    ins.then_inc(feed_lo.sem, 1)
                    if k >= 1:
                        prepare(sec, 24 + k)
                post(sec)

            def cf(sec):
                vec.wait_ge(x_ready.sem, x_ready.at(sec, 0))
                vec.memset(cz[:, :, 0:CFK - 1], 0.0)
                normalise(sec)
                feed_x(sec)
                for j in range(4):
                    vec.wait_ge(sig_ready.sem, sig_ready.at(sec, j + 1))
                    for f in range(2):
                        c = 2 * j + f
                        ins = stt(cz[:, c, CFK - 1:], ps[:, 4 + 2 * j % 4, f * S:(f + 1) * S], gain("bpw1", 0, c),
                                  csg[:, j % 2, f, :], ALU.add, ALU.mult)
                    ins.then_inc(glu_done.sem, 1)
                vec.wait_ge(glu_done.sem, glu_done.at(sec, 4))
                for c in range(KC):
                    n0 = step.mark(ts(ccv[:, c, :], cz[:, c, 0:S], gain("wdw", 0, c), gain("bdw", 0, c), ALU.mult, ALU.add))
                for k in range(1, CFK):
                    for c in range(KC):
                        vec.wait_ge(vec_step, n0 - KC + 1 + c)
                        ins = stt(ccv[:, c, :], cz[:, c, k:k + S], gain("wdw", k, c), ccv[:, c, :], ALU.mult, ALU.add)
                        n1 = step.mark(ins)
                    n0 = n1
                vec.wait_ge(vec_step, n0)
                vec.memset(tmp[:, 0:1], 0.0).then_inc(conv_done.sem, 1)
                vec.wait_ge(conv_T.sem, conv_T.at(sec, 1))
                for t in range(NT):
                    for h in range(2):
                        ins = vec.bn_stats(bns[:, 2 * t + h, :], ps[:, 4 + 2 * t + h, :])
                step.link(ins)
                for t in range(NT):
                    ins = vec.bn_aggr(mv[:, t, :], bns[:, 2 * t:2 * t + 2, :].rearrange("p a b -> p (a b)"))
                ins.then_inc(gn_var.sem, 1)
                vec.wait_ge(gn_rs.sem, gn_rs.at(sec, 1))
                stt(gshift[:, 0:2], mv[:, 0:2, 0], -1.0, grs[:, 0:2], ALU.mult, ALU.mult).then_inc(gn_shift.sem, 1)
                for k in range(4):
                    vec.wait_ge(feed_hi.sem, feed_hi.at(sec, k + 1))
                    tt(u_l[:, k % 2, :, :], csl[:, k % 2, :, :], u_h[:, k % 2, :, :].bitcast(F32), ALU.subtract).then_inc(feed_lo.sem, 1)
                    if k >= 1:
                        prepare(sec, 8 + k)
                vec.wait_ge(used[sec.slot(11)], sec.fill(11) + 1)
                vec.wait_ge(bias_in.sem, bias_in.at(sec, 16))
                for t in range(NT):
                    tt(two(chh[:, t, :]), banks(t), two(cbias), ALU.add).then_inc(hh_ready.sem, 1)
                vec.wait_ge(hh_ready.sem, hh_ready.at(sec, 2))
                post(sec)

            def sc(sec):
                def low(k):
                    vec.wait_ge(feed_hi.sem, feed_hi.at(sec, k + 1))
                    tt(u_l[:, k % 2, :, :], sy[:, k % 2, :, :], u_h[:, k % 2, :, :].bitcast(F32), ALU.subtract).then_inc(feed_lo.sem, 1)

                vec.wait_ge(x_ready.sem, x_ready.at(sec, 0))
                vec.memset(sz[:, :, :, 0:SCK - 1], 0.0)
                normalise(sec)
                feed_x(sec)
                for j in range(4):
                    vec.wait_ge(used[sec.slot(SC_UP[j] + 2)], sec.fill(SC_UP[j] + 2) + 1)
                    vec.wait_ge(gates_sb.sem, gates_sb.at(sec, 2 * j + 2))
                    vec.wait_ge(y_ready.sem, y_ready.at(sec, j))
                    tt(sz[:, j % 2, :, SCK - 1:], ps[:, 4 + (3 * j + 2) % 4, :].rearrange("p (c n) -> p c n", c=2),
                       sgc[:, j % 2, :, :], ALU.mult).then_inc(z_done.sem, 1)
                    vec.wait_ge(z_done.sem, z_done.at(sec, j + 1))
                    for k in range(SCK):
                        for f in range(2):
                            c = 2 * j + f
                            src = sz[:, j % 2, f, k:k + S]
                            if k == 0:
                                ins = ts(scv[:, f, :], src, gain("wconv", k, c), None, ALU.mult)
                            else:
                                ins = stt(scv[:, f, :], src, gain("wconv", k, c), scv[:, f, :], ALU.mult, ALU.add)
                        step.link(ins)
                    vec.wait_ge(feed_lo.sem, feed_lo.at(sec, j - 1))
                    tt(sy[:, j % 2, :, :], scv[:, :, :], sgb[:, j % 2, :, :], ALU.mult).then_inc(y_ready.sem, 1)
                    low(j)
                for c in range(12, 16):
                    prepare(sec, c)
                post(sec)

            def fin(sec):
                vec.wait_ge(rstd_ready.sem, rstd_ready.at(sec, 1))
                vec.wait_ge(row_in.sem, row_in.at(sec, 16))
                for t in range(NT):
                    stt(x[:, t, :], x[:, t, :], rstd[:, t:t + 1], row[:], ALU.mult, ALU.mult).then_inc(x_ready.sem, 1)
                vec.wait_ge(x_ready.sem, x_ready.at(sec, 2))

            vec.wait_ge(pos_in, 16)
            vec.wait_ge(inv_in, 16)
            step.link(vec.tensor_copy(posf, pos_i[:]))
            for t in range(NT):
                ins = ts(s_ang[:, t, :], s_inv, posf[:, t:t + 1], None, ALU.mult)
            step.link(ins)
            magic = 1.5 * 2.0 ** 23
            step.link(ts(s_n, s_ang, 1.0 / (2 * math.pi), magic, ALU.mult, ALU.add))
            step.link(ts(s_n, s_n, magic, None, ALU.subtract))
            src = s_ang
            for part in TWO_PI_PARTS:
                step.link(stt(s_r, s_n, -part, src, ALU.mult, ALU.add))
                src = s_r
            ts(s_r, s_r, -PI_BELOW, PI_BELOW, ALU.max, ALU.min).then_inc(angle_ready, 1)
            vec.wait_ge(lam_in, 32)
            for l in range(DEPTH1):
                for j in range(2):
                    v = lam_rows[:, l, :].rearrange("p (a n) -> p a n", n=CQ)
                    ins = vec.tensor_tensor_reduce(tmp[:, (2 * l + j) * CQ:(2 * l + j + 1) * CQ], v[:, 2 * j, :], v[:, 2 * j + 1, :], 1.0, 0.0, ALU.mult, ALU.add,
                                                   lam4[:, 2 * l + j:2 * l + j + 1])
            ins.then_inc(lam_sum, 1)
            vec.wait_ge(sin_ready, 1)
            step.link(stt(cs[:, :, 0, :], s_n, -2.0, s_n, ALU.mult, ALU.mult))
            ts(cs[:, :, 0, :], cs[:, :, 0, :], 1.0, None, ALU.add)
            vec.wait_ge(lam_exp, 1)
            le = lexp.rearrange("p (l j) -> p l j", j=2)
            step.link(tt(neglam, le[:, :, 1], le[:, :, 0], ALU.subtract))
            for l in range(DEPTH1):
                lam_init = 0.8 - 0.6 * math.exp(-0.3 * l)
                ts(neglam[:, l:l + 1], neglam[:, l:l + 1], lam_init, None, ALU.subtract)
                ins = ts(sub_g[:, l, :], sub_g[:, l, :], 1.0 - lam_init, None, ALU.mult)
            step.link(ins)
            vec.wait_ge(rowsT, 1)
            for c in range(KC):
                n = ROWS_AT[c]
                ins = vec.tensor_copy(gcol[:, c, 0:n], ps[:, c // 4, (c % 4) * P:(c % 4) * P + n])
            ins.then_inc(gains_ready, 1)
            vec.wait_ge(gains_ready, 1)
            vec.wait_ge(rope_in, 16)
            vec.wait_ge(masks_in, 16)
            vec.wait_ge(x_in, 16)
            for sec in sections:
                dict(attn=attn, mlp1=mlp, mlp2=mlp, ret=ret, cf=cf, sc=sc, fin=fin)[sec.kind](sec)


CONSTANTS = ("c_ident", "c_rope", "c_masks", "c_invfreq", "c_decay")
NAMES = ("x", "w_in", "ln1_g", "mla_q_norm_g", "mla_w_uq", "mla_kv_norm_g", "mla_w_ukv", "diff_lambda", "diff_subln_g",
         "w_o", "ln2_g", "w_up", "w_down", "final_g", "positions_2", "norm_g_2", "ret_w_in_2", "ret_gn_g_2",
         "ret_w_out_2", "cf_w_pw1_2", "cf_b_pw1_2", "cf_w_dw_2", "cf_b_dw_2", "cf_ln_g_2", "cf_ln_b_2", "cf_w_pw2_2",
         "cf_b_pw2_2", "sc_w_in_2", "sc_w_conv_2", "sc_w_out_2", "mlp_w1_2", "mlp_w2_2")


def constants():
    import numpy as np
    f = np.float32
    tok = np.arange(S)

    def tables(dim):
        half = dim // 2
        inv = (f(1.0) / (f(10000.0) ** (np.arange(half, dtype=f) / f(half)))).astype(f)
        ang = tok.astype(f)[:, None] * inv[None, :]
        return np.cos(ang).astype(f), np.sin(ang).astype(f)

    rope = np.concatenate([*tables(AD), *tables(CQ)], axis=1).reshape(NT, P, 96).transpose(1, 0, 2)
    dist = tok[:, None] - tok[None, :]
    causal = dist >= 0
    seen = (causal & (dist <= 128)).astype(int) + (causal & (dist % 4 == 0)) + (causal & (dist % 16 == 0))
    dil = np.where(seen > 0, np.log(np.maximum(seen, 1)) * AD ** 0.5, -1e30)
    cau = np.where(causal, 0.0, -1e30)
    masks = np.stack([np.concatenate([m[:P, :P], m[P:, :]], axis=1) for m in (dil, cau)], axis=1)
    lg = np.log1p(-np.exp2(-5.0 - np.arange(RH)))
    dec = [np.where(causal.T, np.exp(g * np.maximum(dist.T, 0)), 0.0) * RDK ** -0.5 for g in lg]
    decay = np.concatenate([np.concatenate([m[:P, :], m[P:, P:]], axis=1) for m in dec], axis=1)
    inv = f(10000.0) ** (-np.arange(0, RDK, 2, dtype=f) / f(RDK))
    return {"c_ident": np.eye(P, dtype=f), "c_rope": np.ascontiguousarray(rope, dtype=f),
            "c_masks": np.ascontiguousarray(masks, dtype=f), "c_invfreq": inv.astype(f)[None],
            "c_decay": np.ascontiguousarray(decay, dtype=f)}


def kernel(**inputs):
    import numpy as np
    import concourse.bacc as bacc
    from concourse.bass_utils import run_bass_kernel_spmd

    nc = bacc.Bacc("TRN2", target_bir_lowering=False, num_devices=1)
    arrays, aps = {}, {}
    for name, v in [(n, inputs[n]) for n in NAMES] + list(constants().items()):
        v = np.ascontiguousarray(v)
        arrays[name + "_dram"] = v
        aps[name] = nc.dram_tensor(name + "_dram", v.shape, mybir.dt.from_np(v.dtype), kind="ExternalInput").ap()
    out = nc.dram_tensor("out_dram", (1, S, D), F32, kind="ExternalOutput").ap()
    build(nc, aps, out)
    r = run_bass_kernel_spmd(nc, [arrays], core_ids=[0])
    return r.results[0]["out_dram"]
```

```python
from contextlib import ExitStack
import math

import concourse.bass as bass
from concourse import mybir

F32 = mybir.dt.float32
F32R = mybir.dt.float32r
I32 = mybir.dt.int32
ALU = mybir.AluOpType
ACT = mybir.ActivationFunctionType
AX = mybir.AxisListType

P = 128
D = 1024
S = 256
NT = S // P
KC = D // P
FF = 4 * D
DEPTH1, DEPTH2 = 2, 4
AH, AD = 6, 64
BH, BN, BR, BV = 6, 64, 32, 64
BQ, BKV = 384, 128
CH, CQ, CV = 4, 32, 64
IN_COLS = 3 * AH * AD + BQ + BKV + BR + 2 * CH * 2 * CQ + CH * CV
QA, KA, VA = 0, AH * AD, 2 * AH * AD
CQ0 = 3 * AH * AD
CKV0 = CQ0 + BQ
KR0 = CKV0 + BKV
QC0 = KR0 + BR
KC0 = QC0 + 2 * CH * CQ
VC0 = KC0 + 2 * CH * CQ
GROUPS = (2, 3, 0, 1, 4)
UQ, UKV, LAST_A, LAST_B = 8, 10, 9, 11
RH, RDK, RDV = 4, 256, 512
CFK, SCK = 31, 3
EPS, SUB_EPS, LN_EPS = 1e-6, 1e-5, 1e-5
BQD = BN + BR

RING = 4
CONV_VEC, CONV_POOL, CONV_PE = (0, 2, 3, 4, 5), 1, (6, 7)
AHEAD = 3
TW = 2048
STEPS = FF // 256
LOOPS = (STEPS - 4) // 2

ROWS = {}
_n = 0
for _name, _count in (("ln1", 2), ("ln2", 2), ("norm", 16), ("gn", 4), ("bpw1", 2), ("wdw", CFK), ("bdw", 1),
                      ("lng", 1), ("lnb", 1), ("wconv", SCK), ("qn", 2), ("kvn", 2)):
    ROWS[_name] = _n
    _n += _count
N_ROWS = _n
ROWS_AT = [N_ROWS if c == 0 else ROWS["kvn"] if c < BQ // P else ROWS["qn"] for c in range(KC)]

TWO_PI_PARTS = (6.28125, 0.00193500518798828125, 3.0199159795e-07)
PI_BELOW = 3.1415925

SECTIONS = ([("attn", 0), ("mlp1", 0), ("attn", 1), ("mlp1", 1), ("fin", 0)]
            + [(k, i) for i, m in enumerate(("ret", "cf", "sc", "ret")) for k in (m, "mlp2")])
TILES = {"attn": 16, "mlp1": 32, "mlp2": 32, "fin": 0, "ret": 32, "cf": 12, "sc": 16}
MAPS = AH + 2 * CH + BH
B_FIRST = 3
C_START = AH + B_FIRST
C_END = C_START + 2 * CH
OUT_ORDER = (0, 3, 1, 2)
SC_UP = (0, 3, 7, 11)
SC_OUT = (6, 10, 14, 15)

FEED = dict(attn=1, mlp1=1, mlp2=1, ret=1, cf=1, sc=1)


def times(n, kinds):
    return {k: n for k in kinds.split()}


ALL = "attn mlp1 mlp2 ret cf sc"
POST = "mlp2 ret cf sc"
class Section:
    def __init__(self, index):
        self.kind, self.layer = SECTIONS[index]
        self.index = index
        self.tile0 = sum(TILES[k] for k, _ in SECTIONS[:index])
        self.tiles = TILES[self.kind]

    def slot(self, c):
        return (self.tile0 + c) % RING

    def fill(self, c, i=0):
        return i + (self.tile0 + c) // RING


class Stage:

    def __init__(self, sem, incs):
        self.sem = sem
        self.base = [sum(incs.get(k, 0) for k, _ in SECTIONS[:i]) for i in range(len(SECTIONS) + 1)]

    def at(self, sec, n):
        v = n + self.base[sec.index]
        return max(v, 0) if isinstance(v, int) else v


class Chain:

    def __init__(self, eng, sem):
        self.eng, self.sem, self.n = eng, sem, 0

    def mark(self, ins):
        ins.then_inc(self.sem, 1)
        self.n += 1
        return self.n

    def link(self, ins):
        self.eng.wait_ge(self.sem, self.mark(ins))


N_TILES = sum(TILES[k] for k, _ in SECTIONS)


def owner(t):
    for i in range(len(SECTIONS)):
        sec = Section(i)
        if t < sec.tile0 + sec.tiles:
            return "vector" if sec.kind.startswith("mlp") and t % 2 == 0 else "gpsimd"


def build(nc, a, out):
    ctx = ExitStack()
    with ctx:
        def sb(name, shape, dt=F32):
            return ctx.enter_context(nc.sbuf_tensor(name, shape, dt))

        def sem(name):
            return ctx.enter_context(nc.semaphore(name))

        w_raw = sb("w_raw", [P, RING, TW])
        w_hi = sb("w_hi", [P, RING, TW], F32R)
        w_lo = sb("w_lo", [P, RING, TW], F32R)
        x = sb("x_res", [P, NT, D])
        xT_h = sb("xT_h", [P, KC, S], F32R)
        xT_l = sb("xT_l", [P, KC, S], F32R)
        u_h = sb("u_h", [P, 2, 2, S], F32R)
        u_l = sb("u_l", [P, 2, 2, S], F32R)
        arena = sb("arena", [P, 16384])
        ident = sb("ident", [P, P])
        rope = sb("rope", [P, NT, 96])
        masks = sb("masks", [P, 2, 384])
        gcol = sb("gcol", [P, KC, N_ROWS])
        row = sb("row", [P, D])
        cs = sb("cs", [P, NT, 2, 128])
        lam_rows = sb("lam_rows", [P, DEPTH1, 4 * CQ])
        sub_g = sb("sub_g", [P, DEPTH1, CV])
        st = sb("st", [P, 96])
        pos_i = sb("pos_i", [P, NT], I32)
        ps = ctx.enter_context(nc.psum_tensor("ps", [P, 8, 512], F32))

        def region(start, *shape):
            n = math.prod(shape)
            v = arena[:, start:start + n]
            if len(shape) == 2:
                return v.rearrange("p (a b) -> p a b", a=shape[0])
            if len(shape) == 3:
                return v.rearrange("p (a b c) -> p a b c", a=shape[0], b=shape[1])
            return v

        junk = region(14336, 1024)
        tmp, tmp2 = region(15360, 1024), region(0, 1024)
        rows = region(0, 1024)
        s_ang, s_n, s_r, s_inv = region(1024, NT, 128), region(1280, NT, 128), region(1536, NT, 128), region(1792, 128)
        s_prod = region(1920, 128)
        pr = region(0, NT, IN_COLS)
        o = NT * IN_COLS
        qb = region(o, NT, BH, BQD)
        kb = region(o + NT * BH * BQD, NT, BH, BQD)
        vb = region(o + 2 * NT * BH * BQD, NT, BH, BV)
        mixed = region(8000, NT, D)
        qkT = region(10048, 2, 512)
        sm = region(11072, 2, 384)
        pT = region(11840, 2, 384)
        rope_a, rope_b = region(12608, 768), region(13376, 768)
        relu = region(1024, 2, 512)
        sq = region(2048, 2, 512)
        rqk = region(0, NT, 2048)
        rv = region(4096, NT, 2048)
        rqkT = region(8192, 16, S)
        rg = region(12288, NT, 2048)
        rST = region(0, RH, 384)
        rD = region(1536, RH, 384)
        ry = region(8192, NT, 2048)
        rope_ra = [region(8192 + 2048 * i, 8, 128) for i in range(2)]
        rope_rb = [region(8192 + 2048 * i + 1024, 8, 128) for i in range(2)]
        xn = region(0, NT, D)
        cz = region(2048, KC, CFK - 1 + S)
        csg = region(4352, 2, 2, S)
        ccv = region(5376, KC, S)
        ch = region(7424, NT, D)
        csl = region(9472, 2, 2, S)
        cbias = region(10496, D)
        chh = region(11520, NT, D)
        codd, ptap = region(1024, S), region(1024 + S, 2, S)

        def cdiag(d):
            at = 7424 + P * d if d < 54 else P * (d - 54)
            return arena[:, at:at + P]

        sgb, sgc = region(2048, 2, 2, S), region(3072, 2, 2, S)
        sz = region(4096, 2, 2 * (S + SCK - 1)).rearrange("p a (c n) -> p a c n", c=2)
        scv = region(5248, 2, S)
        sy = region(5760, 2, 2, S)

        ss, ms, rstd, r2 = st[:, 0:2], st[:, 2:4], st[:, 4:6], st[:, 6:8]
        pss, pms, prs, coef = st[:, 76:80], st[:, 10:12], st[:, 12:14], st[:, 14:16]
        lss, lms, lrs = st[:, 16:20], st[:, 20:24], st[:, 24:28]
        negmax, zsum, rz = st[:, 28:32], st[:, 32:36], st[:, 36:40]
        sss, sms, srs = st[:, 40:48], st[:, 48:56], st[:, 56:64]
        lam4, lexp, neglam = st[:, 64:68], st[:, 68:72], st[:, 72:74]
        posf = st[:, 74:76]
        mv = sb("mv", [P, RH * NT, 2])
        gvar, grs, gshift = sb("gvar", [P, 8]), sb("grs", [P, 8]), sb("gshift", [P, 8])
        bns = sb("bns", [P, 4, 6])
        mhalf = sb("mhalf", [P, 8])

        raw_in = [sem(f"raw_in{i}") for i in range(RING)]
        hi_ready = [sem(f"hi_ready{i}") for i in range(RING)]
        lo_ready = [sem(f"lo_ready{i}") for i in range(RING)]
        used = [sem(f"used{i}") for i in range(RING)]
        x_ready = Stage(sem("x_ready"), times(2, ALL + " fin"))
        ss_ready = Stage(sem("ss_ready"), times(2, ALL + " fin"))
        rstd_ready = Stage(sem("rstd_ready"), times(2, ALL + " fin"))
        xn_ready = Stage(sem("xn_ready"), times(2, "cf sc"))
        xT_ready = Stage(sem("xT_ready"), times(4, ALL))
        xT_hi = Stage(sem("xT_hi"), times(8, ALL))
        xT_lo = Stage(sem("xT_lo"), times(8, ALL))
        evac_a = Stage(sem("evac_a"), {"attn": 5, "ret": 12})
        evac_v = Stage(sem("evac_v"), {"attn": 5, "ret": 8})
        feed_T = Stage(sem("feed_T"), {"attn": 4, "ret": 8, "cf": 4})
        feed_hi = Stage(sem("feed_hi"), {"attn": 4, "mlp1": 16, "mlp2": 16, "ret": 8, "cf": 4, "sc": 4})
        feed_lo = Stage(sem("feed_lo"), {"attn": 4, "mlp1": 16, "mlp2": 16, "ret": 8, "cf": 4, "sc": 4})
        row_in = Stage(sem("row_in"), times(16, POST + " fin"))
        acc_ready = Stage(sem("acc_ready"), times(3, ALL))
        post_ss = Stage(sem("post_ss"), times(4, POST))
        post_rs = Stage(sem("post_rs"), times(2, POST))
        relu_done = Stage(sem("relu_done"), {"mlp1": 16, "mlp2": 16})
        sq_done = Stage(sem("sq_done"), {"mlp1": 16, "mlp2": 16})
        lat_T = Stage(sem("lat_T"), {"attn": 2})
        lat_hi = Stage(sem("lat_hi"), {"attn": 4})
        lat_lo = Stage(sem("lat_lo"), {"attn": 4})
        lat_ss = Stage(sem("lat_ss"), {"attn": 1})
        lat_rs = Stage(sem("lat_rs"), {"attn": 1})
        q_done = Stage(sem("q_done"), {"attn": 1})
        kv_done = Stage(sem("kv_done"), {"attn": 1})
        rope_done = Stage(sem("rope_done"), {"attn": 1, "ret": 4})
        rope_p = Stage(sem("rope_p"), {"attn": 2})
        qkT_ready = Stage(sem("qkT_ready"), {"attn": MAPS})
        qkT_sb = Stage(sem("qkT_sb"), {"attn": MAPS})
        scores_ready = Stage(sem("scores_ready"), {"attn": MAPS})
        max_ready = Stage(sem("max_ready"), {"attn": MAPS})
        probs_ready = Stage(sem("probs_ready"), {"attn": MAPS})
        pT_ready = Stage(sem("pT_ready"), {"attn": MAPS})
        pT_sb = Stage(sem("pT_sb"), {"attn": MAPS})
        pv_ready = Stage(sem("pv_ready"), {"attn": MAPS})
        head_done = Stage(sem("head_done"), {"attn": MAPS})
        sub_ss = Stage(sem("sub_ss"), {"attn": 1})
        sub_rs = Stage(sem("sub_rs"), {"attn": 1})
        sub_done = Stage(sem("sub_done"), {"attn": 1})
        qk_T = Stage(sem("qk_T"), {"ret": 8})
        qk_a = Stage(sem("qk_a"), {"ret": 4})
        qk_v = Stage(sem("qk_v"), {"ret": 4})
        decay_in = Stage(sem("decay_in"), {"ret": 16})
        ret_scores = Stage(sem("ret_scores"), {"ret": RH})
        ret_decayed = Stage(sem("ret_decayed"), {"ret": RH})
        ret_pv = Stage(sem("ret_pv"), {"ret": RH})
        gn_var = Stage(sem("gn_var"), {"ret": RH, "cf": 1})
        gn_rs = Stage(sem("gn_rs"), {"ret": RH, "cf": 1})
        gn_shift = Stage(sem("gn_shift"), {"ret": RH, "cf": 1})
        y_normed = Stage(sem("y_normed"), {"ret": RH, "cf": 2})
        y_gated = Stage(sem("y_gated"), {"ret": RH})
        sig_ready = Stage(sem("sig_ready"), {"cf": 4})
        glu_done = Stage(sem("glu_done"), {"cf": 4})
        conv_v = Stage(sem("conv_v"), {"cf": 1})
        conv_p = Stage(sem("conv_p"), {"cf": 1})
        conv_e = Stage(sem("conv_e"), {"cf": len(CONV_PE)})
        conv_a = Stage(sem("conv_a"), {"cf": len(CONV_PE)})
        diag_ready = Stage(sem("diag_ready"), {"cf": len(CONV_PE)})
        conv_T = Stage(sem("conv_T"), {"cf": 1})
        silu_done = Stage(sem("silu_done"), {"cf": 4})
        bias_in = Stage(sem("bias_in"), {"cf": 16})
        hh_ready = Stage(sem("hh_ready"), {"cf": 4})
        gates_sb = Stage(sem("gates_sb"), {"sc": 8})
        z_done = Stage(sem("z_done"), {"sc": 4})
        y_ready = Stage(sem("y_ready"), {"sc": 4})
        x_in, ident_in, rope_in, masks_in = sem("x_in"), sem("ident_in"), sem("rope_in"), sem("masks_in")
        rows_in, pos_in, lam_in, inv_in = sem("rows_in"), sem("pos_in"), sem("lam_in"), sem("inv_in")
        rowsT, gains_ready = sem("rowsT"), sem("gains_ready")
        angle_ready, sin_ready, lam_sum, lam_exp = sem("angle_ready"), sem("sin_ready"), sem("lam_sum"), sem("lam_exp")
        cos_ready = sem("cos_ready")
        halves_ready = sem("halves_ready")
        vec_step, pool_step, act_step = sem("vec_step"), sem("pool_step"), sem("act_step")
        stored = sem("stored")

        sections = [Section(i) for i in range(len(SECTIONS))]

        def gain(name, index, c):
            r = ROWS[name] + index
            return gcol[:, c, r:r + 1]

        def banks(t):
            return ps[:, 2 * t:2 * t + 2, :]

        def two(v):
            return v.rearrange("p (a b) -> p a b", a=2)

        def head(m):
            if m < AH:
                return (pr[:, :, QA + m * AD:QA + (m + 1) * AD], pr[:, :, KA + m * AD:KA + (m + 1) * AD],
                        pr[:, :, VA + m * AD:VA + (m + 1) * AD], AD, AD ** -0.5, 0)
            if not C_START <= m < C_END:
                m = latent(m)
                return qb[:, :, m, :], kb[:, :, m, :], vb[:, :, m, :], BQD, BQD ** -0.5, 1
            m -= C_START
            return (pr[:, :, QC0 + m * CQ:QC0 + (m + 1) * CQ], pr[:, :, KC0 + m * CQ:KC0 + (m + 1) * CQ],
                    pr[:, :, VC0 + m // 2 * CV:VC0 + (m // 2 + 1) * CV], CQ, CQ ** -0.5, 1)

        def latent(m):
            return m - AH if m < C_START else m - AH - 2 * CH

        def mixed_head(m):
            c = 64 * (m if m < AH else AH + BH + (m - C_START) // 2 if C_START <= m < C_END else AH + latent(m))
            return mixed[:, :, c:c + 64]

        def row_load(name, src, n=D):
            r = ROWS[name]
            return rows[r:r + src.shape[0], 0:n], src, rows_in

        gn = a["ret_gn_g_2"].rearrange("l (h n) -> (l h) n", n=D)
        row_loads = [row_load("ln1", a["ln1_g"]), row_load("ln2", a["ln2_g"]),
                     row_load("norm", a["norm_g_2"].rearrange("l r n -> (l r) n")), row_load("gn", gn),
                     row_load("bpw1", a["cf_b_pw1_2"].rearrange("l (h n) -> (l h) n", n=D)), row_load("wdw", a["cf_w_dw_2"][0]),
                     row_load("bdw", a["cf_b_dw_2"]), row_load("lng", a["cf_ln_g_2"]), row_load("lnb", a["cf_ln_b_2"]),
                     row_load("wconv", a["sc_w_conv_2"][0]), row_load("qn", a["mla_q_norm_g"], BQ),
                     row_load("kvn", a["mla_kv_norm_g"], BKV)]

        def tiles_of(sec):
            l = sec.layer
            if sec.kind == "attn":
                w = a["w_in"][l].rearrange("(h c p) n -> h p c n", h=2, p=P)
                for g in GROUPS[:4]:
                    for h in range(2):
                        yield w[h, :, :, 512 * g:512 * g + 512]
                yield a["mla_w_uq"][l].rearrange("(c p) n -> p c n", p=P)
                yield w[0, :, :, 2048:IN_COLS]
                yield a["mla_w_ukv"][l].rearrange("(c p) n -> p c n", p=P)
                yield w[1, :, :, 2048:IN_COLS]
                steps = list(down_tiles(a["w_o"][l], D))
                for k in OUT_ORDER:
                    yield steps[k]
            elif sec.kind == "ret":
                w = a["ret_w_in_2"][l // 3].rearrange("(h c p) n -> h p c n", h=2, p=P)
                for g in range(12):
                    for h in range(2):
                        yield w[h, :, :, 512 * g:512 * g + 512]
                yield from down_tiles(a["ret_w_out_2"][l // 3], 2 * D)
            elif sec.kind == "cf":
                w = a["cf_w_pw1_2"][0].rearrange("(c p) n -> p c n", p=P)
                for n in range(8):
                    c = (n % 2) * D + (n // 2) * 256
                    yield w[:, :, c:c + 256]
                yield from down_tiles(a["cf_w_pw2_2"][0], D)
            elif sec.kind == "sc":
                w = a["sc_w_in_2"][0].rearrange("(c p) n -> p c n", p=P)
                outs = list(down_tiles(a["sc_w_out_2"][0], D))
                for n in range(16):
                    if n in SC_OUT:
                        yield outs[SC_OUT.index(n)]
                    else:
                        j = max(i for i in range(4) if SC_UP[i] <= n)
                        c = (n - SC_UP[j]) * D + j * 256
                        yield w[:, :, c:c + 256]

        def down_tiles(w, k):
            for s in range(k // 256):
                yield w[256 * s:256 * s + 256, :].rearrange("(c p) n -> p c n", p=P)

        block = ctx.enter_context(nc.Block())

        @block.sync
        def _(sp):
            def load(sec, c, view, i=0):
                slot, fill = sec.slot(c), sec.fill(c, i)
                sp.wait_ge(lo_ready[slot], fill)
                n = view.shape[1] * view.shape[2]
                dst = w_raw[:, slot, 0:n].rearrange("p (c n) -> p c n", c=view.shape[1])
                sp.dma_start(dst, view).then_inc(raw_in[slot], 16)

            def mlp(sec):
                first = sec.kind == "mlp1"
                up = (a["w_up"] if first else a["mlp_w1_2"])[sec.layer].rearrange("(c p) n -> p c n", p=P)
                down = (a["w_down"] if first else a["mlp_w2_2"])[sec.layer].rearrange("(s c p) n -> s p c n", c=2, p=P)

                def up_tile(k):
                    return up[:, :, bass.ds(k * 256, 256)]

                def down_tile(k):
                    return down[bass.ds(k, 1)].rearrange("a p c n -> p (a c) n")

                load(sec, 0, up_tile(0))
                load(sec, 1, up_tile(1))
                load(sec, 2, down_tile(0))
                with sp.Fori(0, LOOPS) as i:
                    load(sec, 3, up_tile(i * 2 + 2), i)
                    load(sec, 4, down_tile(i * 2 + 1), i)
                    load(sec, 5, up_tile(i * 2 + 3), i)
                    load(sec, 6, down_tile(i * 2 + 2), i)
                load(sec, 27, up_tile(STEPS - 2))
                load(sec, 28, down_tile(STEPS - 3))
                load(sec, 29, up_tile(STEPS - 1))
                load(sec, 30, down_tile(STEPS - 2))
                load(sec, 31, down_tile(STEPS - 1))

            for dst, src, s in (*row_loads[6:],
                                (lam_rows[:].rearrange("p l n -> p (l n)"), a["diff_lambda"].rearrange("(o l) a b -> o (l a b)", o=1).to_broadcast([P, DEPTH1 * 4 * CQ]), lam_in),
                                (sub_g[:].rearrange("p l n -> p (l n)"), a["diff_subln_g"].rearrange("(o l) n -> o (l n)", o=1).to_broadcast([P, DEPTH1 * CV]), lam_in)):
                sp.dma_start(dst, src).then_inc(s, 16)
            sp.dma_start(x[:], a["x"][0].rearrange("(t p) n -> p t n", p=P)).then_inc(x_in, 16)
            for sec in sections:
                if sec.kind.startswith("mlp"):
                    mlp(sec)
                else:
                    for c, view in enumerate(tiles_of(sec)):
                        load(sec, c, view)
            last = sections[-1]
            sp.wait_ge(x_ready.sem, x_ready.at(last, 2))
            sp.dma_start(out[0].rearrange("(t p) n -> p t n", p=P), x[:]).then_inc(stored, 16)
            sp.wait_ge(stored, 16)

        @block.tensor
        def _(pe):
            def tile_ready(sec, c, i=0):
                slot = sec.slot(c)
                pe.wait_ge(lo_ready[slot], sec.fill(c, i) + 1)
                return slot

            def three(dst, lh, ll, rh, rl, start, stop):
                pe.matmul(dst, lh, rh, start=start, stop=False)
                pe.matmul(dst, lh, rl, start=False, stop=False)
                return pe.matmul(dst, ll, rh, start=False, stop=stop)

            def feed_x(sec):
                for t in range(NT):
                    if sec.kind in ("cf", "sc"):
                        src = xn
                        pe.wait_ge(xn_ready.sem, xn_ready.at(sec, t + 1))
                    else:
                        src = x
                        pe.wait_ge(x_ready.sem, x_ready.at(sec, t - 1))
                    for b in range(4):
                        for j in range(2):
                            c = 2 * b + j
                            ins = pe.transpose(ps[:, 4 + b, j * S + t * P:j * S + (t + 1) * P],
                                               src[:, t, c * P:(c + 1) * P], ident[:])
                        if t == 1:
                            ins.then_inc(xT_ready.sem, 1)

            def wide(sec, c, n, h, bank0):
                slot = tile_ready(sec, c)
                for kl in range(4):
                    kc = 4 * h + kl
                    if c < 2:
                        pe.wait_ge(xT_lo.sem, xT_lo.at(sec, kc + 1))
                    for t in range(NT):
                        wsl = slice(kl * n, kl * n + n)
                        ins = three(ps[:, bank0 + t, 0:n], xT_h[:, kc, t * P:(t + 1) * P], xT_l[:, kc, t * P:(t + 1) * P],
                                    w_hi[:, slot, wsl], w_lo[:, slot, wsl], kc == 0, kc == KC - 1)
                ins.then_inc(used[slot], 1)

            def up(sec, bank, c, i=0, first=False):
                slot = tile_ready(sec, c, i)
                for f in range(2):
                    for kc in range(KC):
                        if first and f == 0:
                            pe.wait_ge(xT_lo.sem, xT_lo.at(sec, max(kc + 1, 2)))
                        wsl = slice(kc * 256 + f * P, kc * 256 + (f + 1) * P)
                        ins = three(ps[:, bank, f * S:(f + 1) * S], w_hi[:, slot, wsl], w_lo[:, slot, wsl],
                                    xT_h[:, kc, :], xT_l[:, kc, :], kc == 0, kc == KC - 1)
                ins.then_inc(used[slot], 1)

            def down(sec, k, us, c, i=0, first=False, last=False):
                pe.wait_ge(feed_lo.sem, feed_lo.at(sec, k + 1))
                slot = tile_ready(sec, c, i)

                def part(cc, t, h):
                    wsl = slice(cc * D + h * 512, cc * D + h * 512 + 512)
                    return three(ps[:, 2 * t + h, :], u_h[:, us, cc, t * P:(t + 1) * P], u_l[:, us, cc, t * P:(t + 1) * P],
                                 w_hi[:, slot, wsl], w_lo[:, slot, wsl], first and cc == 0, last and cc == 1)

                if last:
                    for b in range(4):
                        part(0, b // 2, b % 2)
                        ins = part(1, b // 2, b % 2)
                        if b < 3:
                            ins.then_inc(acc_ready.sem, 1)
                        else:
                            ins.then_inc(used[slot], 1)
                else:
                    for cc in range(2):
                        for t in range(NT):
                            for h in range(2):
                                ins = part(cc, t, h)
                    ins.then_inc(used[slot], 1)

            def turn_step(sec, k, src, at):
                for c in range(2):
                    for t in range(NT):
                        ins = pe.transpose(ps[:, 4 + k % 2, c * S + t * P:c * S + (t + 1) * P],
                                           src[:, t, (2 * at + c) * P:(2 * at + c + 1) * P], ident[:])
                ins.then_inc(feed_T.sem, 1)

            def out_steps(sec, n, tile0, src, ready, order=None):
                for k in range(n + 1):
                    if k < n:
                        ready(k)
                        if k >= 2:
                            pe.wait_ge(feed_lo.sem, feed_lo.at(sec, k - 1))
                        turn_step(sec, k, src, order[k] if order else k)
                    if k >= 1:
                        down(sec, k - 1, (k - 1) % 2, tile0 + k - 1, first=k == 1, last=k == n)

            def mlp(sec):
                def up_k(k, par, c, i=0):
                    pe.wait_ge(relu_done.sem, relu_done.at(sec, k - 1))
                    up(sec, 4 + par, c, i)

                feed_x(sec)
                up(sec, 4, 0, first=True)
                up(sec, 5, 1)
                down(sec, 0, 0, 2, first=True)
                with pe.Fori(0, LOOPS) as i:
                    up_k(i * 2 + 2, 0, 3, i)
                    down(sec, i * 2 + 1, 1, 4, i)
                    up_k(i * 2 + 3, 1, 5, i)
                    down(sec, i * 2 + 2, 0, 6, i)
                up_k(STEPS - 2, 0, 27)
                down(sec, STEPS - 3, 1, 28)
                up_k(STEPS - 1, 1, 29)
                down(sec, STEPS - 2, 0, 30)
                down(sec, STEPS - 1, 1, 31, last=True)

            def attn(sec):
                feed_x(sec)
                def latents():
                    pe.wait_ge(evac_a.sem, evac_a.at(sec, 2))
                    pe.wait_ge(evac_v.sem, evac_v.at(sec, 2))
                    for b in range(2):
                        for j in range(2):
                            for t in range(NT):
                                c0 = CQ0 + (2 * b + j) * P
                                ins = pe.transpose(ps[:, 4 + b, j * S + t * P:j * S + (t + 1) * P],
                                                   pr[:, t, c0:c0 + P], ident[:])
                        ins.then_inc(lat_T.sem, 1)

                for p in range(4):
                    if p >= 2:
                        pe.wait_ge(evac_a.sem, evac_a.at(sec, p - 1))
                        pe.wait_ge(evac_v.sem, evac_v.at(sec, p - 1))
                    wide(sec, 2 * p, 512, 0, 2 * (p % 2))
                    if p == 2:
                        latents()
                    wide(sec, 2 * p + 1, 512, 1, 2 * (p % 2))
                pe.wait_ge(lat_lo.sem, lat_lo.at(sec, 4))
                slot = tile_ready(sec, UQ)
                n, half = BH * BQD, BH * BQD // 2
                for t in range(NT):
                    for h in range(2):
                        for c in range(BQ // P):
                            wsl = slice(c * n + h * half, c * n + (h + 1) * half)
                            tok = slice(t * P, (t + 1) * P)
                            ins = three(ps[:, 4 + 2 * t + h, 0:half], u_h[:, c // 2, c % 2, tok], u_l[:, c // 2, c % 2, tok],
                                        w_hi[:, slot, wsl], w_lo[:, slot, wsl], c == 0, c == BQ // P - 1)
                ins.then_inc(used[slot], 1)
                pe.wait_ge(evac_a.sem, evac_a.at(sec, 3))
                pe.wait_ge(evac_v.sem, evac_v.at(sec, 3))
                wide(sec, LAST_A, IN_COLS - 2048, 0, 0)
                pe.wait_ge(q_done.sem, q_done.at(sec, 1))
                slot = tile_ready(sec, UKV)
                half = BH * (BN + BV) // 2
                for t in range(NT):
                    for h in range(2):
                        wsl = slice(h * half, (h + 1) * half)
                        tok = slice(t * P, (t + 1) * P)
                        ins = three(ps[:, 4 + 2 * t + h, 0:half], u_h[:, 1, 1, tok], u_l[:, 1, 1, tok],
                                    w_hi[:, slot, wsl], w_lo[:, slot, wsl], True, True)
                ins.then_inc(used[slot], 1)
                wide(sec, LAST_B, IN_COLS - 2048, 1, 0)
                pe.wait_ge(kv_done.sem, kv_done.at(sec, 1))
                pe.wait_ge(rope_done.sem, rope_done.at(sec, 1))
                for s in range(MAPS + 3):
                    if s == 2:
                        pe.wait_ge(evac_a.sem, evac_a.at(sec, 5))
                        pe.wait_ge(evac_v.sem, evac_v.at(sec, 5))
                    if s == AH:
                        pe.wait_ge(rope_p.sem, rope_p.at(sec, 1))
                    if s == C_START:
                        pe.wait_ge(rope_p.sem, rope_p.at(sec, 2))
                    if s < MAPS:
                        m = s
                        q, k, _, d, _, _ = head(m)
                        pe.wait_ge(qkT_sb.sem, qkT_sb.at(sec, m - 1))
                        for j, v in enumerate((q, k)):
                            for t in range(NT):
                                ins = pe.transpose(ps[0:d, 4 + m % 2, j * S + t * P:j * S + (t + 1) * P], v[:, t, :], ident[:])
                        ins.then_inc(qkT_ready.sem, 1)
                    m = s - 1
                    if 0 <= m < MAPS:
                        d = head(m)[3]
                        pe.wait_ge(qkT_sb.sem, qkT_sb.at(sec, m + 1))
                        pe.wait_ge(max_ready.sem, max_ready.at(sec, m - 1))
                        pe.matmul(ps[:, 6 + m % 2, 0:P], qkT[0:d, m % 2, 0:P], qkT[0:d, m % 2, S:S + P], start=True, stop=True)
                        pe.matmul(ps[:, 6 + m % 2, P:P + S], qkT[0:d, m % 2, P:S], qkT[0:d, m % 2, S:2 * S],
                                  start=True, stop=True).then_inc(scores_ready.sem, 1)
                    m = s - 2
                    if 0 <= m < MAPS:
                        pe.wait_ge(probs_ready.sem, probs_ready.at(sec, m + 1))
                        pe.wait_ge(pT_sb.sem, pT_sb.at(sec, m - 1))
                        for j in range(3):
                            ins = pe.transpose(ps[:, m % 2, j * P:(j + 1) * P], sm[:, m % 2, j * P:(j + 1) * P], ident[:])
                        ins.then_inc(pT_ready.sem, 1)
                    m = s - 3
                    if m >= 0:
                        v = head(m)[2]
                        pe.wait_ge(pT_sb.sem, pT_sb.at(sec, m + 1))
                        pe.wait_ge(head_done.sem, head_done.at(sec, m - 1))
                        pe.matmul(ps[:, 2 + m % 2, 0:64], pT[:, m % 2, 0:P], v[:, 0, :], start=True, stop=True)
                        pe.matmul(ps[:, 2 + m % 2, 64:128], pT[:, m % 2, P:2 * P], v[:, 0, :], start=True, stop=False)
                        pe.matmul(ps[:, 2 + m % 2, 64:128], pT[:, m % 2, 2 * P:3 * P], v[:, 1, :], start=False,
                                  stop=True).then_inc(pv_ready.sem, 1)

                def ready(k):
                    if k == 1:
                        pe.wait_ge(sub_done.sem, sub_done.at(sec, 1))
                        pe.wait_ge(head_done.sem, head_done.at(sec, MAPS))

                out_steps(sec, 4, 12, mixed, ready, OUT_ORDER)

            def ret(sec):
                def group(g):
                    if g >= 2:
                        pe.wait_ge(evac_a.sem, evac_a.at(sec, g - 1))
                        pe.wait_ge(evac_v.sem, evac_v.at(sec, min(g - 1, 8)))
                    for h in range(2):
                        wide(sec, 2 * g + h, 512, h, 2 * (g % 2))

                def pv(h):
                    if h >= 2:
                        pe.wait_ge(y_normed.sem, y_normed.at(sec, h - 1))
                    b = 4 + 2 * (h % 2)
                    pe.matmul(ps[:, b, :], rST[:, h, 0:P], rv[:, 0, h * RDV:(h + 1) * RDV], start=True, stop=True)
                    pe.matmul(ps[:, b + 1, :], rST[:, h, P:S], rv[:, 0, h * RDV:(h + 1) * RDV], start=True, stop=False)
                    pe.matmul(ps[:, b + 1, :], rST[:, h, S:S + P], rv[:, 1, h * RDV:(h + 1) * RDV], start=False,
                              stop=True).then_inc(ret_pv.sem, 1)

                feed_x(sec)
                for g in range(8):
                    group(g)
                pe.wait_ge(rope_done.sem, rope_done.at(sec, 4))
                for b in range(8):
                    if b >= 4:
                        pe.wait_ge((qk_a if b % 2 == 0 else qk_v).sem, (qk_a if b % 2 == 0 else qk_v).at(sec, b // 2 - 1))
                    for j in range(2):
                        for t in range(NT):
                            c = 2 * b + j
                            ins = pe.transpose(ps[:, 4 + b % 4, j * S + t * P:j * S + (t + 1) * P],
                                               rqk[:, t, c * P:(c + 1) * P], ident[:])
                    ins.then_inc(qk_T.sem, 1)
                group(8)
                pe.wait_ge(qk_a.sem, qk_a.at(sec, 4))
                pe.wait_ge(qk_v.sem, qk_v.at(sec, 4))
                for h in range(RH):
                    for kt in range(2):
                        for c in range(2):
                            cq, ck = 2 * h + c, 8 + 2 * h + c
                            dst = ps[:, 4 + h, 0:S] if kt == 0 else ps[:, 4 + h, S:S + P]
                            ins = pe.matmul(dst, rqkT[:, ck, kt * P:(kt + 1) * P], rqkT[:, cq, kt * P:S], start=c == 0, stop=c == 1)
                    ins.then_inc(ret_scores.sem, 1)
                group(9)
                pe.wait_ge(evac_v.sem, evac_v.at(sec, 8))
                pe.wait_ge(ret_decayed.sem, ret_decayed.at(sec, RH))
                pv(0)
                pv(1)
                group(10)
                pv(2)
                pv(3)
                group(11)

                def ready(k):
                    if k == 0:
                        pe.wait_ge(y_normed.sem, y_normed.at(sec, RH))
                    if k == 1:
                        pe.wait_ge(evac_a.sem, evac_a.at(sec, 12))
                    pe.wait_ge(y_gated.sem, y_gated.at(sec, k // 2 + 1))

                out_steps(sec, 8, 24, ry, ready)

            def cf(sec):
                feed_x(sec)
                for n in range(8):
                    if n >= 4:
                        pe.wait_ge(glu_done.sem, glu_done.at(sec, n // 2 - 1))
                    up(sec, 4 + n % 4, n, first=n == 0)
                pe.wait_ge(glu_done.sem, glu_done.at(sec, 4))
                for n, c in enumerate(CONV_PE):
                    pe.wait_ge(diag_ready.sem, diag_ready.at(sec, n + 1))
                    for k in range(CFK):
                        ins = pe.matmul(ps[:, n, 0:S], cdiag(CFK * n + k), cz[:, c, k:k + S], start=k == 0, stop=k == CFK - 1)
                    ins.then_inc(conv_e.sem, 1)
                pe.wait_ge(conv_v.sem, conv_v.at(sec, 1))
                pe.wait_ge(conv_p.sem, conv_p.at(sec, 1))
                pe.wait_ge(conv_a.sem, conv_a.at(sec, len(CONV_PE)))
                for c in range(KC):
                    for t in range(NT):
                        ins = pe.transpose(ps[:, 4 + 2 * t + c // 4, (c % 4) * P:(c % 4 + 1) * P], ccv[:, c, t * P:(t + 1) * P], ident[:])
                ins.then_inc(conv_T.sem, 1)
                pe.wait_ge(y_normed.sem, y_normed.at(sec, 2))
                out_steps(sec, 4, 8, ch, lambda k: None)

            def sc(sec):
                feed_x(sec)
                for j in range(4):
                    for q in range(3):
                        m = 3 * j + q
                        if m >= 4:
                            jj, qq = divmod(m - 4, 3)
                            if qq == 2:
                                pe.wait_ge(z_done.sem, z_done.at(sec, jj + 1))
                            else:
                                pe.wait_ge(gates_sb.sem, gates_sb.at(sec, 2 * jj + qq + 1))
                        up(sec, 4 + m % 4, SC_UP[j] + q, first=m == 0)
                    if j >= 1:
                        down(sec, j - 1, (j - 1) % 2, SC_OUT[j - 1], first=j == 1)
                down(sec, 3, 1, SC_OUT[3], last=True)

            pe.wait_ge(ident_in, 16)
            pe.wait_ge(rows_in, 16 * len(row_loads))
            for c in range(KC):
                n = ROWS_AT[c]
                ins = pe.transpose(ps[:, c // 4, (c % 4) * P:(c % 4) * P + n], rows[0:n, c * P:(c + 1) * P], ident[0:n, 0:n])
            ins.then_inc(rowsT, 1)
            pe.wait_ge(x_in, 16)
            for sec in sections:
                if sec.kind != "fin":
                    dict(attn=attn, mlp1=mlp, mlp2=mlp, ret=ret, cf=cf, sc=sc)[sec.kind](sec)

        @block.scalar
        def _(act):
            def prepare(sec, c, i=0):
                if sec.tile0 + c + AHEAD >= N_TILES:
                    return
                slot, fill = sec.slot(c + AHEAD), sec.fill(c + AHEAD, i)
                act.wait_ge(raw_in[slot], fill * 16 + 16)
                act.wait_ge(used[slot], fill)
                act.activation(w_hi[:, slot, :], w_raw[:, slot, :], ACT.Copy).then_inc(hi_ready[slot], 1)

            def load_row(sec):
                i = sec.layer
                src = (a["final_g"].rearrange("(a n) -> a n", a=1) if sec.kind == "fin"
                       else a["norm_g_2"][i, 3:4] if sec.kind == "mlp2" else a["norm_g_2"][i, 1:2])
                act.dma_start(row[:], src.to_broadcast([P, D])).then_inc(row_in.sem, 16)

            def start(sec):
                act.wait_ge(post_ss.sem, post_ss.at(sec, 0))
                for t in range(NT):
                    act.wait_ge(x_ready.sem, x_ready.at(sec, t - 1))
                    act.activation((junk, tmp)[t], x[:, t, :], ACT.Square, accum_out=ss[:, t:t + 1]).then_inc(ss_ready.sem, 1)
                if sec.kind not in ("attn", "mlp1"):
                    load_row(sec)

            def feed_x(sec):
                for b in range(4):
                    act.wait_ge(xT_ready.sem, xT_ready.at(sec, b + 1))
                    for j in range(2):
                        c = 2 * b + j
                        name, idx = (("ln1", sec.layer) if sec.kind == "attn" else ("ln2", sec.layer) if sec.kind == "mlp1"
                                     else ("norm", 4 * sec.layer + (2 if sec.kind == "mlp2" else 0)))
                        act.activation(xT_h[:, c, :], ps[:, 4 + b, j * S:(j + 1) * S], ACT.Copy,
                                       scale=gain(name, idx, c)).then_inc(xT_hi.sem, 1)

            def post(sec, last_tile):
                for b in range(4):
                    act.wait_ge(post_ss.sem, post_ss.at(sec, b - 1))
                    scale = r2[:, b // 2:b // 2 + 1] if sec.kind == "mlp2" else 1.0
                    if sec.kind == "cf":
                        act.wait_ge(hh_ready.sem, hh_ready.at(sec, b + 1))
                        src = chh[:, b // 2, b % 2 * 512:(b % 2 + 1) * 512]
                    elif b < 3:
                        act.wait_ge(acc_ready.sem, acc_ready.at(sec, b + 1))
                        src = ps[:, b, :]
                    else:
                        act.wait_ge(used[sec.slot(last_tile)], sec.fill(last_tile) + 1)
                        src = ps[:, b, :]
                    act.activation(two(junk)[:, b % 2, :], src, ACT.Square, scale=scale,
                                   accum_out=pss[:, b:b + 1]).then_inc(post_ss.sem, 1)

            def mlp(sec):
                def square(k, par, c, i=0):
                    act.wait_ge(relu_done.sem, relu_done.at(sec, k + 1))
                    act.wait_ge(feed_lo.sem, feed_lo.at(sec, k - 1))
                    act.activation(sq[:, par, :], relu[:, par, :], ACT.Square).then_inc(sq_done.sem, 1)
                    act.wait_ge(sq_done.sem, sq_done.at(sec, k + 1))

                def high(k, par):
                    act.activation(u_h[:, par, :, :].rearrange("p a b -> p (a b)"), sq[:, par, :], ACT.Copy).then_inc(feed_hi.sem, 1)

                feed_x(sec)
                start(sec)
                prepare(sec, 0)
                square(0, 0, 0)
                high(0, 0)
                prepare(sec, 1)
                square(1, 1, 1)
                high(1, 1)
                prepare(sec, 2)
                with act.Fori(0, LOOPS) as i:
                    for par in range(2):
                        prepare(sec, 3 + 2 * par, i)
                        square(i * 2 + 2 + par, par, None)
                        act.wait_ge(used[sec.slot(2 if par == 0 else 4)], sec.fill(2 if par == 0 else 4, i) + 1)
                        high(i * 2 + 2 + par, par)
                        prepare(sec, 4 + 2 * par, i)
                for par in range(2):
                    prepare(sec, 27 + 2 * par)
                    square(STEPS - 2 + par, par, None)
                    act.wait_ge(used[sec.slot(26 + 2 * par)], sec.fill(26 + 2 * par) + 1)
                    high(STEPS - 2 + par, par)
                    prepare(sec, 28 + 2 * par)
                prepare(sec, 31)
                if sec.kind == "mlp2":
                    post(sec, 31)

            def evac(sec, g, n=512):
                tile = LAST_B if sec.kind == "attn" and g == 4 else 2 * g + 1
                act.wait_ge(used[sec.slot(tile)], sec.fill(tile) + 1)
                b = 2 * (g % 2)
                if sec.kind == "attn":
                    c = 512 * GROUPS[g]
                    ins = act.activation(pr[:, 0, c:c + n], ps[:, b, 0:n], ACT.Copy, scale=rstd[:, 0:1])
                elif g < 8:
                    dst = rqk[:, 0, 512 * g:512 * g + 512] if g < 4 else rv[:, 0, 512 * (g - 4):512 * (g - 3)]
                    ins = act.activation(dst, ps[:, b, :], ACT.Copy, scale=rstd[:, 0:1])
                else:
                    for t in range(NT):
                        ins = act.activation(rg[:, t, 512 * (g - 8):512 * (g - 7)], ps[:, b + t, :], ACT.Silu, scale=rstd[:, t:t + 1])
                ins.then_inc(evac_a.sem, 1)

            def angles():
                act.wait_ge(angle_ready, 1)
                act.activation(cs[:, :, 1, :], s_r, ACT.Sin)
                act.activation(s_n, s_r, ACT.Sin, scale=0.5).then_inc(sin_ready, 1)
                act.wait_ge(lam_sum, 1)
                act.activation(lexp, lam4, ACT.Exp).then_inc(lam_exp, 1)
                act.wait_ge(cos_ready, 1)

            def attn(sec):
                feed_x(sec)
                if sec.index == 0:
                    for c in range(1, AHEAD):
                        prepare(sec, c - AHEAD)
                start(sec)
                if sec.index == 0:
                    angles()
                act.wait_ge(rstd_ready.sem, rstd_ready.at(sec, 2))
                for p in range(4):
                    prepare(sec, 2 * p)
                    if p > 0:
                        evac(sec, p - 1)
                    if p == 2:
                        for c in range(4):
                            act.wait_ge(lat_T.sem, lat_T.at(sec, c // 2 + 1))
                            act.activation(u_h[:, c // 2, c % 2, :], ps[:, 4 + c // 2, (c % 2) * S:(c % 2 + 1) * S], ACT.Copy,
                                           scale=gain("qn" if c < 3 else "kvn", sec.layer, c % 3)).then_inc(lat_hi.sem, 1)
                        act.wait_ge(evac_v.sem, evac_v.at(sec, 2))
                        for j, (c0, n) in enumerate(((CQ0, BQ), (CKV0, BKV))):
                            for t in range(NT):
                                ins = act.activation(junk[:, j * 768 + t * n:j * 768 + (t + 1) * n], pr[:, t, c0:c0 + n],
                                                     ACT.Square, accum_out=lss[:, 2 * j + t:2 * j + t + 1])
                        ins.then_inc(lat_ss.sem, 1)
                    prepare(sec, 2 * p + 1)
                prepare(sec, 8)
                evac(sec, 3)
                act.wait_ge(used[sec.slot(UQ)], sec.fill(UQ) + 1)
                act.wait_ge(lat_rs.sem, lat_rs.at(sec, 1))
                for t in range(NT):
                    for h in range(2):
                        n = BH * BQD // 2
                        ins = act.activation(qb[:, t, :, :].rearrange("p h d -> p (h d)")[:, h * n:(h + 1) * n],
                                             ps[:, 4 + 2 * t + h, 0:n], ACT.Copy, scale=lrs[:, t:t + 1])
                ins.then_inc(q_done.sem, 1)
                prepare(sec, 9)
                prepare(sec, 10)
                prepare(sec, 11)
                evac(sec, 4, IN_COLS - 2048)
                prepare(sec, 12)
                for s in range(MAPS + 1):
                    if s < MAPS:
                        m = s
                        act.wait_ge(qkT_ready.sem, qkT_ready.at(sec, m + 1))
                        act.wait_ge(scores_ready.sem, scores_ready.at(sec, m - 1))
                        d = head(m)[3]
                        act.activation(qkT[0:d, m % 2, :], ps[0:d, 4 + m % 2, :], ACT.Copy).then_inc(qkT_sb.sem, 1)
                    m = s - 1
                    if 0 <= m < MAPS:
                        scale = head(m)[4]
                        act.wait_ge(max_ready.sem, max_ready.at(sec, m + 1))
                        for t in range(NT):
                            c = slice(0, P) if t == 0 else slice(P, P + S)
                            j = 2 * (m % 2) + t
                            ins = act.activation(sm[:, m % 2, c], sm[:, m % 2, c], ACT.Exp, bias=negmax[:, j:j + 1], scale=-1.0,
                                                 accum_out=zsum[:, j:j + 1])
                        ins.then_inc(probs_ready.sem, 1)
                for k in range(4):
                    act.wait_ge(feed_T.sem, feed_T.at(sec, k + 1))
                    if k >= 2:
                        act.wait_ge(used[sec.slot(12 + k - 2)], sec.fill(12 + k - 2) + 1)
                    act.activation(u_h[:, k % 2, :, :].rearrange("p a b -> p (a b)"), ps[:, 4 + k % 2, :], ACT.Copy).then_inc(feed_hi.sem, 1)
                    if k >= 1:
                        prepare(sec, 12 + k)

            def ret(sec):
                def norm(h):
                    act.wait_ge(gn_shift.sem, gn_shift.at(sec, h + 1))
                    for t in range(NT):
                        j = 2 * h + t
                        ins = act.activation(ry[:, t, h * RDV:(h + 1) * RDV], ps[:, 4 + 2 * (h % 2) + t, :], ACT.Identity,
                                             scale=grs[:, j:j + 1], bias=gshift[:, j:j + 1])
                    ins.then_inc(y_normed.sem, 1)

                feed_x(sec)
                start(sec)
                act.wait_ge(rstd_ready.sem, rstd_ready.at(sec, 2))
                for g in range(8):
                    prepare(sec, 2 * g)
                    if g > 0:
                        evac(sec, g - 1, 512)
                    prepare(sec, 2 * g + 1)
                prepare(sec, 16)
                evac(sec, 7, 512)
                for b in range(0, 8, 2):
                    act.wait_ge(qk_T.sem, qk_T.at(sec, b + 1))
                    act.activation(rqkT[:, 2 * b:2 * b + 2, :].rearrange("p a b -> p (a b)"), ps[:, 4 + b % 4, :],
                                   ACT.Copy).then_inc(qk_a.sem, 1)
                act.wait_ge(qk_T.sem, qk_T.at(sec, 8))
                act.dma_start(rD.rearrange("p h n -> p (h n)"), a["c_decay"]).then_inc(decay_in.sem, 16)
                prepare(sec, 17)
                prepare(sec, 18)
                evac(sec, 8, 512)
                prepare(sec, 19)
                prepare(sec, 20)
                evac(sec, 9, 512)
                norm(0)
                norm(1)
                prepare(sec, 21)
                prepare(sec, 22)
                evac(sec, 10, 512)
                norm(2)
                norm(3)
                prepare(sec, 23)
                prepare(sec, 24)
                evac(sec, 11, 512)
                for k in range(8):
                    act.wait_ge(feed_T.sem, feed_T.at(sec, k + 1))
                    if k >= 2:
                        act.wait_ge(used[sec.slot(24 + k - 2)], sec.fill(24 + k - 2) + 1)
                    for c in range(2):
                        g = 2 * (sec.layer // 3) + (2 * k + c) // 8
                        ins = act.activation(u_h[:, k % 2, c, :], ps[:, 4 + k % 2, c * S:(c + 1) * S], ACT.Copy,
                                             scale=gain("gn", g, (2 * k + c) % 8))
                    ins.then_inc(feed_hi.sem, 1)
                    if k >= 1:
                        prepare(sec, 24 + k)
                post(sec, 31)

            def cf(sec):
                start(sec)
                feed_x(sec)
                for j in range(4):
                    prepare(sec, 2 * j)
                    prepare(sec, 2 * j + 1)
                    act.wait_ge(used[sec.slot(2 * j + 1)], sec.fill(2 * j + 1) + 1)
                    act.wait_ge(glu_done.sem, glu_done.at(sec, j - 1))
                    for f in range(2):
                        c = 2 * j + f
                        ins = act.activation(csg[:, j % 2, f, :], ps[:, 4 + (2 * j + 1) % 4, f * S:(f + 1) * S], ACT.Sigmoid,
                                             bias=gain("bpw1", 1, c))
                    ins.then_inc(sig_ready.sem, 1)
                    n_diag = len(CONV_PE) * CFK
                    for d in range(j * n_diag // 4, (j + 1) * n_diag // 4):
                        ins = act.activation(cdiag(d), ident[:], ACT.Copy, scale=gain("wdw", d % CFK, CONV_PE[d // CFK]))
                        if d % CFK == CFK - 1:
                            ins.then_inc(diag_ready.sem, 1)
                prepare(sec, 8)
                for n, c in enumerate(CONV_PE):
                    act.wait_ge(conv_e.sem, conv_e.at(sec, n + 1))
                    act.activation(ccv[:, c, :], ps[:, n, 0:S], ACT.Identity, bias=gain("bdw", 0, c)).then_inc(conv_a.sem, 1)
                act.dma_start(cbias, a["cf_b_pw2_2"].to_broadcast([P, D])).then_inc(bias_in.sem, 16)
                act.wait_ge(gn_shift.sem, gn_shift.at(sec, 1))
                for t in range(NT):
                    act.activation(two(ch[:, t, :]), ps[:, 4 + 2 * t:6 + 2 * t, :], ACT.Identity, scale=grs[:, t:t + 1],
                                   bias=gshift[:, t:t + 1]).then_inc(y_normed.sem, 1)
                for k in range(4):
                    act.wait_ge(feed_T.sem, feed_T.at(sec, k + 1))
                    act.wait_ge(feed_lo.sem, feed_lo.at(sec, k - 1))
                    for f in range(2):
                        c = 2 * k + f
                        ins = act.activation(csl[:, k % 2, f, :], ps[:, 4 + k % 2, f * S:(f + 1) * S], ACT.Silu,
                                             scale=gain("lng", 0, c), bias=gain("lnb", 0, c))
                    ins.then_inc(silu_done.sem, 1)
                    act.wait_ge(silu_done.sem, silu_done.at(sec, k + 1))
                    if k >= 2:
                        act.wait_ge(used[sec.slot(8 + k - 2)], sec.fill(8 + k - 2) + 1)
                    act.activation(u_h[:, k % 2, :, :], csl[:, k % 2, :, :], ACT.Copy).then_inc(feed_hi.sem, 1)
                    if k >= 1:
                        prepare(sec, 8 + k)
                post(sec, 11)

            def sc(sec):
                def high(k):
                    act.wait_ge(y_ready.sem, y_ready.at(sec, k + 1))
                    if k >= 2:
                        act.wait_ge(used[sec.slot(SC_OUT[k - 2])], sec.fill(SC_OUT[k - 2]) + 1)
                    act.activation(u_h[:, k % 2, :, :], sy[:, k % 2, :, :], ACT.Copy).then_inc(feed_hi.sem, 1)

                start(sec)
                feed_x(sec)
                for n in range(16):
                    prepare(sec, n)
                    if n in SC_OUT:
                        continue
                    j = max(i for i in range(4) if SC_UP[i] <= n)
                    q = n - SC_UP[j]
                    if q < 2:
                        act.wait_ge(used[sec.slot(n)], sec.fill(n) + 1)
                        act.wait_ge(y_ready.sem, y_ready.at(sec, j - 1))
                        act.wait_ge(z_done.sem, z_done.at(sec, j - 1))
                        dst = (sgb, sgc)[q]
                        act.activation(dst[:, j % 2, :, :].rearrange("p a b -> p (a b)"), ps[:, 4 + (3 * j + q) % 4, :],
                                       ACT.Copy).then_inc(gates_sb.sem, 1)
                    if q == 0 and j > 0:
                        high(j - 1)
                    if n == SC_UP[3] + 2:
                        high(3)
                post(sec, 15)

            for dst, src, s in ((ident[:], a["c_ident"], ident_in), *row_loads[:6],
                                (pos_i[:], a["positions_2"][0].rearrange("(t p) -> p t", p=P), pos_in),
                                (s_inv, a["c_invfreq"].to_broadcast([P, 128]), inv_in),
                                (rope[:], a["c_rope"], rope_in), (masks[:], a["c_masks"], masks_in)):
                with nc.allow_non_contiguous_dma(reason="256 positions"):
                    act.dma_start(dst, src).then_inc(s, 16)
            prepare(sections[0], -AHEAD)
            act.wait_ge(x_in, 16)
            act.wait_ge(gains_ready, 1)
            for sec in sections:
                dict(attn=attn, mlp1=mlp, mlp2=mlp, ret=ret, cf=cf, sc=sc, fin=start)[sec.kind](sec)

        def rotate(eng, step, v, h, half, cos, sin, ra, rb):
            shape = [P, h, 2, half]
            v4 = v.rearrange("p h (a d) -> p h a d", a=2)
            ra4 = ra.rearrange("p (h a d) -> p h a d", h=h, a=2)
            rb4 = rb.rearrange("p (h a d) -> p h a d", h=h, a=2)
            eng.tensor_tensor(ra4, v4, cos.unsqueeze(1).unsqueeze(1).to_broadcast(shape), ALU.mult)
            step.link(eng.tensor_tensor(rb4, v4, sin.unsqueeze(1).unsqueeze(1).to_broadcast(shape), ALU.mult))
            eng.tensor_tensor(v4[:, :, 0, :], ra4[:, :, 0, :], rb4[:, :, 1, :], ALU.subtract)
            return eng.tensor_tensor(v4[:, :, 1, :], rb4[:, :, 0, :], ra4[:, :, 1, :], ALU.add)

        @block.gpsimd
        def _(pool):
            step = Chain(pool, pool_step)

            def prepare(sec, c, i=0):
                t = sec.tile0 + c + AHEAD
                if t < N_TILES and owner(t) == "gpsimd":
                    slot = sec.slot(c + AHEAD)
                    pool.wait_ge(hi_ready[slot], sec.fill(c + AHEAD, i) + 1)
                    pool.tensor_tensor(w_lo[:, slot, :], w_raw[:, slot, :], w_hi[:, slot, :].bitcast(F32),
                                       ALU.subtract).then_inc(lo_ready[slot], 1)

            def rsqrt(dst, mid, src, n, scale, eps):
                step.link(pool.tensor_scalar(mid, src, scale, eps, ALU.mult, ALU.add))
                return pool.tensor_tensor(dst, mid, mhalf[:, 0:n], ALU.pow)

            def start(sec):
                for t in range(NT):
                    pool.wait_ge(ss_ready.sem, ss_ready.at(sec, t + 1))
                    rsqrt(rstd[:, t:t + 1], ms[:, t:t + 1], ss[:, t:t + 1], 1, 1.0 / D, EPS).then_inc(rstd_ready.sem, 1)

            def post(sec):
                for t in range(NT):
                    pool.wait_ge(post_ss.sem, post_ss.at(sec, 2 * t + 2))
                    step.link(pool.tensor_tensor(pms[:, t:t + 1], pss[:, 2 * t:2 * t + 1], pss[:, 2 * t + 1:2 * t + 2], ALU.add))
                    rsqrt(prs[:, t:t + 1], pms[:, t:t + 1], pms[:, t:t + 1], 1, 1.0 / D, EPS).then_inc(post_rs.sem, 1)

            def mlp(sec):
                start(sec)
                for c in range(3):
                    prepare(sec, c)
                with pool.Fori(0, LOOPS) as i:
                    for c in range(3, 7):
                        prepare(sec, c, i)
                for c in range(27, 32):
                    prepare(sec, c)
                if sec.kind == "mlp2":
                    post(sec)

            def attn(sec):
                start(sec)
                for c in range(5):
                    prepare(sec, c)
                pool.wait_ge(lat_ss.sem, lat_ss.at(sec, 1))
                step.link(pool.tensor_scalar(lms[:, 0:2], lss[:, 0:2], 1.0 / BQ, EPS, ALU.mult, ALU.add))
                step.link(pool.tensor_scalar(lms[:, 2:4], lss[:, 2:4], 1.0 / BKV, EPS, ALU.mult, ALU.add))
                pool.tensor_tensor(lrs, lms, mhalf[:, 0:4], ALU.pow).then_inc(lat_rs.sem, 1)
                for c in range(5, 13):
                    prepare(sec, c)
                pool.wait_ge(q_done.sem, q_done.at(sec, 1))
                pool.wait_ge(rope_done.sem, rope_done.at(sec, 1))
                for t in range(NT):
                    ins = rotate(pool, step, qb[:, t, :, BN:BQD], BH, BR // 2, rope[:, t, 64:80], rope[:, t, 80:96],
                                 rope_a[:, 0:BH * BR], rope_b[:, 0:BH * BR])
                    if t == 0:
                        step.link(ins)
                    else:
                        ins.then_inc(rope_p.sem, 1)
                pool.wait_ge(rope_p.sem, rope_p.at(sec, 1))
                pool.wait_ge(evac_a.sem, evac_a.at(sec, 5))
                pool.wait_ge(evac_v.sem, evac_v.at(sec, 5))
                for t in range(NT):
                    ins = rotate(pool, step, pr[:, t, QC0:VC0].rearrange("p (h d) -> p h d", d=CQ), 4 * CH, CQ // 2,
                                 rope[:, t, 64:80], rope[:, t, 80:96], rope_a[:, 0:512], rope_b[:, 0:512])
                    if t == 0:
                        step.link(ins)
                    else:
                        ins.then_inc(rope_p.sem, 1)
                pool.wait_ge(sub_ss.sem, sub_ss.at(sec, 1))
                rsqrt(srs, sms, sss, 8, 1.0 / CV, SUB_EPS).then_inc(sub_rs.sem, 1)
                for c in range(13, 16):
                    prepare(sec, c)

            def ret(sec):
                def var(h):
                    pool.wait_ge(gn_var.sem, gn_var.at(sec, h + 1))
                    j = 2 * h
                    rsqrt(grs[:, j:j + 2], gvar[:, j:j + 2], mv[:, j:j + 2, 1], 2, 1.0, LN_EPS).then_inc(gn_rs.sem, 1)

                start(sec)
                for c in range(21):
                    prepare(sec, c)
                var(0)
                var(1)
                for c in range(21, 23):
                    prepare(sec, c)
                var(2)
                var(3)
                for c in range(23, 32):
                    prepare(sec, c)
                post(sec)

            def cf(sec):
                start(sec)
                for c in range(5):
                    prepare(sec, c)
                pool.wait_ge(glu_done.sem, glu_done.at(sec, CONV_POOL // 2 + 1))
                c = CONV_POOL
                step.link(pool.tensor_scalar(ccv[:, c, :], cz[:, c, 0:S], gain("wdw", 0, c), gain("bdw", 0, c), ALU.mult, ALU.add))
                step.link(pool.tensor_scalar(ptap[:, 1, :], cz[:, c, 1:1 + S], gain("wdw", 1, c), 0.0, ALU.mult, ALU.add))
                for k in range(1, CFK):
                    if k + 1 < CFK:
                        step.mark(pool.tensor_scalar(ptap[:, (k + 1) % 2, :], cz[:, c, k + 1:k + 1 + S],
                                                               gain("wdw", k + 1, c), 0.0, ALU.mult, ALU.add))
                    ins = pool.tensor_tensor(ccv[:, c, :], ccv[:, c, :], ptap[:, k % 2, :], ALU.add)
                    if k + 1 < CFK:
                        step.link(ins)
                    else:
                        ins.then_inc(conv_p.sem, 1)
                for c in range(5, 9):
                    prepare(sec, c)
                pool.wait_ge(gn_var.sem, gn_var.at(sec, 1))
                rsqrt(grs[:, 0:2], gvar[:, 0:2], mv[:, 0:2, 1], 2, 1.0, LN_EPS).then_inc(gn_rs.sem, 1)
                for c in range(9, 12):
                    prepare(sec, c)
                post(sec)

            def sc(sec):
                start(sec)
                for c in range(16):
                    prepare(sec, c)
                post(sec)

            step.link(pool.memset(mhalf[:], -0.5))
            for c in range(AHEAD):
                prepare(sections[0], c - AHEAD)
            for sec in sections:
                dict(attn=attn, mlp1=mlp, mlp2=mlp, ret=ret, cf=cf, sc=sc, fin=start)[sec.kind](sec)

        @block.vector
        def _(vec):
            step = Chain(vec, vec_step)
            tt, ts, stt = vec.tensor_tensor, vec.tensor_scalar, vec.scalar_tensor_tensor

            def prepare(sec, c, i=0):
                t = sec.tile0 + c + AHEAD
                if t < N_TILES and owner(t) == "vector":
                    slot = sec.slot(c + AHEAD)
                    vec.wait_ge(hi_ready[slot], sec.fill(c + AHEAD, i) + 1)
                    vec.tensor_tensor(w_lo[:, slot, :], w_raw[:, slot, :], w_hi[:, slot, :].bitcast(F32),
                                       ALU.subtract).then_inc(lo_ready[slot], 1)

            def feed_x(sec):
                name, idx = (("ln1", sec.layer) if sec.kind == "attn" else ("ln2", sec.layer) if sec.kind == "mlp1"
                             else ("norm", 4 * sec.layer + (2 if sec.kind == "mlp2" else 0)))
                for c in range(KC):
                    vec.wait_ge(xT_hi.sem, xT_hi.at(sec, c // 2 * 2 + 2))
                    stt(xT_l[:, c, :], ps[:, 4 + c // 2, (c % 2) * S:(c % 2 + 1) * S], gain(name, idx, c),
                        xT_h[:, c, :].bitcast(F32), ALU.mult, ALU.subtract).then_inc(xT_lo.sem, 1)

            def normalise(sec):
                for t in range(NT):
                    vec.wait_ge(rstd_ready.sem, rstd_ready.at(sec, t + 1))
                    ts(xn[:, t, :], x[:, t, :], rstd[:, t:t + 1], None, ALU.mult).then_inc(xn_ready.sem, 1)

            def post(sec):
                vec.wait_ge(row_in.sem, row_in.at(sec, 16))
                for t in range(NT):
                    part = (tmp, tmp2)[t]
                    for h in range(2):
                        c = slice(h * 512, (h + 1) * 512)
                        vec.wait_ge(post_ss.sem, post_ss.at(sec, 2 * t + h + 1))
                        src = chh[:, t, c] if sec.kind == "cf" else ps[:, 2 * t + h, :]
                        ins = tt(part[:, c], src, row[:, c], ALU.mult)
                    step.link(ins)
                    vec.wait_ge(post_rs.sem, post_rs.at(sec, t + 1))
                    f = prs[:, t:t + 1]
                    if sec.kind == "mlp2":
                        step.link(tt(coef[:, t:t + 1], prs[:, t:t + 1], r2[:, t:t + 1], ALU.mult))
                        f = coef[:, t:t + 1]
                    stt(x[:, t, :], part, f, x[:, t, :], ALU.mult, ALU.add).then_inc(x_ready.sem, 1)

            def mlp(sec):
                def rectify(k, par, c, i=0):
                    vec.wait_ge(used[sec.slot(c)], sec.fill(c, i) + 1)
                    vec.wait_ge(sq_done.sem, sq_done.at(sec, k - 1))
                    ts(relu[:, par, :], ps[:, 4 + par, :], 0.0, None, ALU.max).then_inc(relu_done.sem, 1)

                def low(k, par):
                    vec.wait_ge(feed_hi.sem, feed_hi.at(sec, k + 1))
                    tt(u_l[:, par, :, :].rearrange("p a b -> p (a b)"), sq[:, par, :],
                       u_h[:, par, :, :].rearrange("p a b -> p (a b)").bitcast(F32), ALU.subtract).then_inc(feed_lo.sem, 1)

                feed_x(sec)
                vec.wait_ge(rstd_ready.sem, rstd_ready.at(sec, 2))
                step.link(vec.reciprocal(r2, ms))
                prepare(sec, 0)
                rectify(0, 0, 0)
                low(0, 0)
                prepare(sec, 1)
                rectify(1, 1, 1)
                low(1, 1)
                prepare(sec, 2)
                with vec.Fori(0, LOOPS) as i:
                    for par in range(2):
                        prepare(sec, 3 + 2 * par, i)
                        rectify(i * 2 + 2 + par, par, 3 + 2 * par, i)
                        low(i * 2 + 2 + par, par)
                        prepare(sec, 4 + 2 * par, i)
                for par in range(2):
                    prepare(sec, 27 + 2 * par)
                    rectify(STEPS - 2 + par, par, 27 + 2 * par)
                    low(STEPS - 2 + par, par)
                    prepare(sec, 28 + 2 * par)
                prepare(sec, 31)
                if sec.kind == "mlp2":
                    post(sec)
                else:
                    for t in range(NT):
                        if t == 0:
                            vec.wait_ge(acc_ready.sem, acc_ready.at(sec, 2))
                        else:
                            vec.wait_ge(used[sec.slot(31)], sec.fill(31) + 1)
                        stt(two(x[:, t, :]), banks(t), r2[:, t:t + 1], two(x[:, t, :]), ALU.mult,
                            ALU.add).then_inc(x_ready.sem, 1)

            def finish_setup():
                vec.wait_ge(sin_ready, 1)
                step.link(stt(cs[:, :, 0, :], s_n, -2.0, s_n, ALU.mult, ALU.mult))
                ts(cs[:, :, 0, :], cs[:, :, 0, :], 1.0, None, ALU.add).then_inc(cos_ready, 1)
                vec.wait_ge(lam_exp, 1)
                le = lexp.rearrange("p (l j) -> p l j", j=2)
                step.link(tt(neglam, le[:, :, 1], le[:, :, 0], ALU.subtract))
                for l in range(DEPTH1):
                    lam_init = 0.8 - 0.6 * math.exp(-0.3 * l)
                    ts(neglam[:, l:l + 1], neglam[:, l:l + 1], lam_init, None, ALU.subtract)
                    ins = ts(sub_g[:, l, :], sub_g[:, l, :], 1.0 - lam_init, None, ALU.mult)
                step.link(ins)

            def attn(sec):
                c64, s64 = [rope[:, t, 0:32] for t in range(NT)], [rope[:, t, 32:64] for t in range(NT)]
                c32, s32 = [rope[:, t, 64:80] for t in range(NT)], [rope[:, t, 80:96] for t in range(NT)]

                def evac(p, n=512):
                    tile = LAST_B if p == 4 else 2 * p + 1
                    vec.wait_ge(used[sec.slot(tile)], sec.fill(tile) + 1)
                    c = 512 * GROUPS[p]
                    ts(pr[:, 1, c:c + n], ps[:, 2 * (p % 2) + 1, 0:n], rstd[:, 1:2], None, ALU.mult).then_inc(evac_v.sem, 1)

                feed_x(sec)
                if sec.index == 0:
                    finish_setup()
                vec.wait_ge(rstd_ready.sem, rstd_ready.at(sec, 2))
                evac(0)
                evac(1)
                for c in range(4):
                    vec.wait_ge(lat_hi.sem, lat_hi.at(sec, c // 2 * 2 + 2))
                    stt(u_l[:, c // 2, c % 2, :], ps[:, 4 + c // 2, (c % 2) * S:(c % 2 + 1) * S],
                        gain("qn" if c < 3 else "kvn", sec.layer, c % 3), u_h[:, c // 2, c % 2, :].bitcast(F32),
                        ALU.mult, ALU.subtract).then_inc(lat_lo.sem, 1)
                vec.wait_ge(evac_a.sem, evac_a.at(sec, 2))
                vec.wait_ge(evac_v.sem, evac_v.at(sec, 2))
                for t in range(NT):
                    step.link(rotate(vec, step, pr[:, t, KR0:KR0 + BR].unsqueeze(1), 1, BR // 2, c32[t], s32[t],
                                     rope_a[:, 0:BR], rope_b[:, 0:BR]))
                for t in range(NT):
                    ins = vec.tensor_copy(kb[:, t, :, BN:BQD], pr[:, t, KR0:KR0 + BR].unsqueeze(1).to_broadcast([P, BH, BR]))
                evac(2)
                evac(3)
                vec.wait_ge(evac_a.sem, evac_a.at(sec, 4))
                vec.wait_ge(evac_v.sem, evac_v.at(sec, 4))
                for t in range(NT):
                    ins = rotate(vec, step, pr[:, t, QA:VA].rearrange("p (h d) -> p h d", d=AD), 2 * AH, AD // 2,
                                 c64[t], s64[t], rope_a, rope_b)
                    if t == 0:
                        step.link(ins)
                    else:
                        ins.then_inc(rope_done.sem, 1)
                for c in range(11):
                    prepare(sec, c)
                vec.wait_ge(used[sec.slot(UKV)], sec.fill(UKV) + 1)
                vec.wait_ge(lat_rs.sem, lat_rs.at(sec, 1))
                for t in range(NT):
                    for h in range(2):
                        kv = ps[:, 4 + 2 * t + h, 0:384].rearrange("p (h d) -> p h d", h=3)
                        ts(kb[:, t, 3 * h:3 * h + 3, 0:BN], kv[:, :, 0:BN], lrs[:, 2 + t:3 + t], None, ALU.mult)
                        ins = ts(vb[:, t, 3 * h:3 * h + 3, :], kv[:, :, BN:BN + BV], lrs[:, 2 + t:3 + t], None, ALU.mult)
                ins.then_inc(kv_done.sem, 1)
                evac(4, IN_COLS - 2048)
                for c in range(11, 13):
                    prepare(sec, c)
                for s in range(1, MAPS + 3):
                    m = s - 1
                    if m < MAPS:
                        scale = head(m)[4]
                        mask = masks[:, head(m)[5], :]
                        vec.wait_ge(scores_ready.sem, scores_ready.at(sec, m + 1))
                        vec.wait_ge(pT_ready.sem, pT_ready.at(sec, m - 1))
                        for t in range(NT):
                            c = slice(0, P) if t == 0 else slice(P, P + S)
                            j = 2 * (m % 2) + t
                            ins = vec.tensor_tensor_reduce(sm[:, m % 2, c], ps[:, 6 + m % 2, c], mask[:, c], -scale, 3.0e38,
                                                           ALU.add, ALU.min, negmax[:, j:j + 1])
                        ins.then_inc(max_ready.sem, 1)
                    m = s - 3
                    if m >= 0:
                        vec.wait_ge(pv_ready.sem, pv_ready.at(sec, m + 1))
                        dst = mixed_head(m)
                        j = 2 * (m % 2)
                        rzb = rz[:, j:j + 2].unsqueeze(2).to_broadcast([P, NT, 64])
                        src = ps[:, 2 + m % 2, 0:128].rearrange("p (t d) -> p t d", t=NT)
                        second = C_START <= m < C_END and (m - C_START) % 2 == 1
                        if not second:
                            tt(dst, src, rzb, ALU.mult).then_inc(head_done.sem, 1)
                        else:
                            t2 = tmp[:, 0:128].rearrange("p (t d) -> p t d", t=NT)
                            step.link(tt(t2, src, rzb, ALU.mult))
                            stt(dst, t2, neglam[:, sec.layer:sec.layer + 1], dst, ALU.mult, ALU.add).then_inc(head_done.sem, 1)
                            vec.wait_ge(head_done.sem, head_done.at(sec, m + 1))
                    m = s - 2
                    if 0 <= m < MAPS:
                        vec.wait_ge(pT_ready.sem, pT_ready.at(sec, m + 1))
                        vec.wait_ge(pv_ready.sem, pv_ready.at(sec, m - 1))
                        vec.tensor_copy(pT[:, m % 2, :], ps[:, m % 2, 0:384]).then_inc(pT_sb.sem, 1)
                        j = 2 * (m % 2)
                        step.link(vec.reciprocal(rz[:, j:j + 2], zsum[:, j:j + 2]))
                    if s == C_END + 2:
                        vec.wait_ge(head_done.sem, head_done.at(sec, C_END))
                        mc = mixed[:, :, D - CH * CV:D]
                        t2 = tmp[:, 0:512].rearrange("p (t n) -> p t n", t=NT)
                        step.link(tt(t2, mc, mc, ALU.mult))
                        vec.tensor_reduce(sss, tmp[:, 0:512].rearrange("p (h d) -> p h d", d=CV), AX.X, ALU.add).then_inc(sub_ss.sem, 1)
                    if s == C_END + 4:
                        vec.wait_ge(sub_rs.sem, sub_rs.at(sec, 1))
                        for t in range(NT):
                            v = mc[:, t, :].rearrange("p (h d) -> p h d", d=CV)
                            step.link(tt(v, v, srs[:, 4 * t:4 * t + 4].unsqueeze(2).to_broadcast([P, CH, CV]), ALU.mult))
                            ins = tt(v, v, sub_g[:, sec.layer, :].unsqueeze(1).to_broadcast([P, CH, CV]), ALU.mult)
                        ins.then_inc(sub_done.sem, 1)
                for k in range(4):
                    vec.wait_ge(feed_hi.sem, feed_hi.at(sec, k + 1))
                    tt(u_l[:, k % 2, :, :].rearrange("p a b -> p (a b)"), ps[:, 4 + k % 2, :],
                       u_h[:, k % 2, :, :].rearrange("p a b -> p (a b)").bitcast(F32), ALU.subtract).then_inc(feed_lo.sem, 1)
                    if k >= 1:
                        prepare(sec, 12 + k)
                for t in range(NT):
                    if t == 0:
                        vec.wait_ge(acc_ready.sem, acc_ready.at(sec, 2))
                    else:
                        vec.wait_ge(used[sec.slot(15)], sec.fill(15) + 1)
                    tt(two(x[:, t, :]), banks(t), two(x[:, t, :]), ALU.add).then_inc(x_ready.sem, 1)

            def ret(sec):
                def evac(g):
                    vec.wait_ge(used[sec.slot(2 * g + 1)], sec.fill(2 * g + 1) + 1)
                    dst = rqk[:, 1, 512 * g:512 * g + 512] if g < 4 else rv[:, 1, 512 * (g - 4):512 * (g - 3)]
                    ts(dst, ps[:, 2 * (g % 2) + 1, :], rstd[:, 1:2], None, ALU.mult).then_inc(evac_v.sem, 1)

                def statistics(h):
                    vec.wait_ge(ret_pv.sem, ret_pv.at(sec, h + 1))
                    for t in range(NT):
                        ins = vec.bn_stats(bns[:, t, :], ps[:, 4 + 2 * (h % 2) + t, :])
                    step.link(ins)
                    for t in range(NT):
                        ins = vec.bn_aggr(mv[:, 2 * h + t, :], bns[:, t, :])
                    ins.then_inc(gn_var.sem, 1)
                    vec.wait_ge(gn_rs.sem, gn_rs.at(sec, h + 1))
                    j = 2 * h
                    stt(gshift[:, j:j + 2], mv[:, j:j + 2, 0], -1.0, grs[:, j:j + 2], ALU.mult, ALU.mult).then_inc(gn_shift.sem, 1)

                def gate(h):
                    vec.wait_ge(y_normed.sem, y_normed.at(sec, h + 1))
                    vec.wait_ge(evac_a.sem, evac_a.at(sec, 8 + h + 1))
                    v = ry[:, :, h * RDV:(h + 1) * RDV]
                    tt(v, v, rg[:, :, h * RDV:(h + 1) * RDV], ALU.mult).then_inc(y_gated.sem, 1)

                feed_x(sec)
                vec.wait_ge(rstd_ready.sem, rstd_ready.at(sec, 2))
                n = 0
                for g in range(8):
                    evac(g)
                    if g in (3, 4, 5, 6):
                        t, j = divmod(g - 3, 2)
                        vec.wait_ge(evac_a.sem, evac_a.at(sec, 4))
                        if g == 3:
                            vec.wait_ge(evac_v.sem, evac_v.at(sec, 4))
                        i = (g - 3) % 2
                        ins = rotate(vec, step, rqk[:, t, j * D:(j + 1) * D].rearrange("p (h d) -> p h d", d=RDK), RH, RDK // 2,
                                     cs[:, t, 0, :], cs[:, t, 1, :], rope_ra[i].rearrange("p a b -> p (a b)"),
                                     rope_rb[i].rearrange("p a b -> p (a b)"))
                        ins.then_inc(rope_done.sem, 1)
                        vec.wait_ge(rope_done.sem, rope_done.at(sec, g - 2))
                for b in range(1, 8, 2):
                    vec.wait_ge(qk_T.sem, qk_T.at(sec, b + 1))
                    vec.tensor_copy(rqkT[:, 2 * b:2 * b + 2, :].rearrange("p a b -> p (a b)"), ps[:, 4 + b % 4, :]).then_inc(qk_v.sem, 1)
                vec.wait_ge(decay_in.sem, decay_in.at(sec, 16))
                for h in range(RH):
                    vec.wait_ge(ret_scores.sem, ret_scores.at(sec, h + 1))
                    tt(rST[:, h, :], ps[:, 4 + h, 0:384], rD[:, h, :], ALU.mult).then_inc(ret_decayed.sem, 1)
                statistics(0)
                statistics(1)
                gate(0)
                gate(1)
                statistics(2)
                statistics(3)
                gate(2)
                for k in range(8):
                    if k == 2:
                        gate(3)
                    vec.wait_ge(feed_hi.sem, feed_hi.at(sec, k + 1))
                    for c in range(2):
                        g = 2 * (sec.layer // 3) + (2 * k + c) // 8
                        ins = stt(u_l[:, k % 2, c, :], ps[:, 4 + k % 2, c * S:(c + 1) * S], gain("gn", g, (2 * k + c) % 8),
                                  u_h[:, k % 2, c, :].bitcast(F32), ALU.mult, ALU.subtract)
                    ins.then_inc(feed_lo.sem, 1)
                    if k >= 1:
                        prepare(sec, 24 + k)
                post(sec)

            def cf(sec):
                vec.wait_ge(x_ready.sem, x_ready.at(sec, 0))
                vec.memset(cz[:, :, 0:CFK - 1], 0.0)
                normalise(sec)
                feed_x(sec)
                def convolve(c):
                    marks = [0, 0]
                    for k in range(CFK):
                        dst = (ccv[:, c, :], codd)[k % 2]
                        if k == 0:
                            ins = ts(dst, cz[:, c, 0:S], gain("wdw", 0, c), gain("bdw", 0, c), ALU.mult, ALU.add)
                        elif k == 1:
                            if odd_free[0]:
                                vec.wait_ge(vec_step, odd_free[0])
                            ins = ts(dst, cz[:, c, 1:1 + S], gain("wdw", 1, c), None, ALU.mult)
                        else:
                            vec.wait_ge(vec_step, marks[k % 2])
                            ins = stt(dst, cz[:, c, k:k + S], gain("wdw", k, c), dst, ALU.mult, ALU.add)
                        marks[k % 2] = step.mark(ins)
                    vec.wait_ge(vec_step, max(marks))
                    ins = tt(ccv[:, c, :], ccv[:, c, :], codd, ALU.add)
                    if c == CONV_VEC[-1]:
                        ins.then_inc(conv_v.sem, 1)
                    else:
                        odd_free[0] = step.mark(ins)

                odd_free = [0]
                def glu(j):
                    vec.wait_ge(sig_ready.sem, sig_ready.at(sec, j + 1))
                    vec.wait_ge(used[sec.slot(2 * j)], sec.fill(2 * j) + 1)
                    for f in range(2):
                        c = 2 * j + f
                        ins = stt(cz[:, c, CFK - 1:], ps[:, 4 + 2 * j % 4, f * S:(f + 1) * S], gain("bpw1", 0, c),
                                  csg[:, j % 2, f, :], ALU.add, ALU.mult)
                    ins.then_inc(glu_done.sem, 1)
                    vec.wait_ge(glu_done.sem, glu_done.at(sec, j + 1))

                glu(0)
                convolve(CONV_VEC[0])
                glu(1)
                convolve(CONV_VEC[1])
                glu(2)
                glu(3)
                for c in CONV_VEC[2:]:
                    convolve(c)
                vec.wait_ge(conv_T.sem, conv_T.at(sec, 1))
                for t in range(NT):
                    for h in range(2):
                        ins = vec.bn_stats(bns[:, 2 * t + h, :], ps[:, 4 + 2 * t + h, :])
                step.link(ins)
                for t in range(NT):
                    ins = vec.bn_aggr(mv[:, t, :], bns[:, 2 * t:2 * t + 2, :].rearrange("p a b -> p (a b)"))
                ins.then_inc(gn_var.sem, 1)
                vec.wait_ge(gn_rs.sem, gn_rs.at(sec, 1))
                stt(gshift[:, 0:2], mv[:, 0:2, 0], -1.0, grs[:, 0:2], ALU.mult, ALU.mult).then_inc(gn_shift.sem, 1)
                for k in range(4):
                    vec.wait_ge(feed_hi.sem, feed_hi.at(sec, k + 1))
                    tt(u_l[:, k % 2, :, :], csl[:, k % 2, :, :], u_h[:, k % 2, :, :].bitcast(F32), ALU.subtract).then_inc(feed_lo.sem, 1)
                    if k >= 1:
                        prepare(sec, 8 + k)
                vec.wait_ge(bias_in.sem, bias_in.at(sec, 16))
                for b in range(4):
                    if b < 3:
                        vec.wait_ge(acc_ready.sem, acc_ready.at(sec, b + 1))
                    else:
                        vec.wait_ge(used[sec.slot(11)], sec.fill(11) + 1)
                    c = slice(b % 2 * 512, (b % 2 + 1) * 512)
                    tt(chh[:, b // 2, c], ps[:, b, :], cbias[:, c], ALU.add).then_inc(hh_ready.sem, 1)
                post(sec)

            def sc(sec):
                def low(k):
                    vec.wait_ge(feed_hi.sem, feed_hi.at(sec, k + 1))
                    tt(u_l[:, k % 2, :, :], sy[:, k % 2, :, :], u_h[:, k % 2, :, :].bitcast(F32), ALU.subtract).then_inc(feed_lo.sem, 1)

                vec.wait_ge(x_ready.sem, x_ready.at(sec, 0))
                vec.memset(sz[:, :, :, 0:SCK - 1], 0.0)
                normalise(sec)
                feed_x(sec)
                for j in range(4):
                    vec.wait_ge(used[sec.slot(SC_UP[j] + 2)], sec.fill(SC_UP[j] + 2) + 1)
                    vec.wait_ge(gates_sb.sem, gates_sb.at(sec, 2 * j + 2))
                    vec.wait_ge(y_ready.sem, y_ready.at(sec, j))
                    tt(sz[:, j % 2, :, SCK - 1:], ps[:, 4 + (3 * j + 2) % 4, :].rearrange("p (c n) -> p c n", c=2),
                       sgc[:, j % 2, :, :], ALU.mult).then_inc(z_done.sem, 1)
                    vec.wait_ge(z_done.sem, z_done.at(sec, j + 1))
                    for k in range(SCK):
                        for f in range(2):
                            c = 2 * j + f
                            src = sz[:, j % 2, f, k:k + S]
                            if k == 0:
                                ins = ts(scv[:, f, :], src, gain("wconv", k, c), None, ALU.mult)
                            else:
                                ins = stt(scv[:, f, :], src, gain("wconv", k, c), scv[:, f, :], ALU.mult, ALU.add)
                        step.link(ins)
                    vec.wait_ge(feed_lo.sem, feed_lo.at(sec, j - 1))
                    tt(sy[:, j % 2, :, :], scv[:, :, :], sgb[:, j % 2, :, :], ALU.mult).then_inc(y_ready.sem, 1)
                    low(j)
                for c in range(12, 16):
                    prepare(sec, c)
                post(sec)

            def fin(sec):
                vec.wait_ge(row_in.sem, row_in.at(sec, 16))
                for t in range(NT):
                    vec.wait_ge(rstd_ready.sem, rstd_ready.at(sec, t + 1))
                    stt(x[:, t, :], x[:, t, :], rstd[:, t:t + 1], row[:], ALU.mult, ALU.mult).then_inc(x_ready.sem, 1)
                vec.wait_ge(x_ready.sem, x_ready.at(sec, 2))

            vec.wait_ge(rowsT, 1)
            for c in range(KC):
                n = ROWS_AT[c]
                ins = vec.tensor_copy(gcol[:, c, 0:n], ps[:, c // 4, (c % 4) * P:(c % 4) * P + n])
            ins.then_inc(gains_ready, 1)
            vec.wait_ge(pos_in, 16)
            vec.wait_ge(inv_in, 16)
            step.link(vec.tensor_copy(posf, pos_i[:]))
            for t in range(NT):
                ins = ts(s_ang[:, t, :], s_inv, posf[:, t:t + 1], None, ALU.mult)
            step.link(ins)
            magic = 1.5 * 2.0 ** 23
            step.link(ts(s_n, s_ang, 1.0 / (2 * math.pi), magic, ALU.mult, ALU.add))
            step.link(ts(s_n, s_n, magic, None, ALU.subtract))
            src = s_ang
            for part in TWO_PI_PARTS:
                step.link(stt(s_r, s_n, -part, src, ALU.mult, ALU.add))
                src = s_r
            ts(s_r, s_r, -PI_BELOW, PI_BELOW, ALU.max, ALU.min).then_inc(angle_ready, 1)
            vec.wait_ge(lam_in, 32)
            for l in range(DEPTH1):
                for j in range(2):
                    v = lam_rows[:, l, :].rearrange("p (a n) -> p a n", n=CQ)
                    ins = vec.tensor_tensor_reduce(s_prod[:, (2 * l + j) * CQ:(2 * l + j + 1) * CQ], v[:, 2 * j, :], v[:, 2 * j + 1, :], 1.0, 0.0, ALU.mult, ALU.add,
                                                   lam4[:, 2 * l + j:2 * l + j + 1])
            ins.then_inc(lam_sum, 1)
            vec.wait_ge(gains_ready, 1)
            vec.wait_ge(rope_in, 16)
            vec.wait_ge(masks_in, 16)
            vec.wait_ge(x_in, 16)
            for sec in sections:
                dict(attn=attn, mlp1=mlp, mlp2=mlp, ret=ret, cf=cf, sc=sc, fin=fin)[sec.kind](sec)


CONSTANTS = ("c_ident", "c_rope", "c_masks", "c_invfreq", "c_decay")
NAMES = ("x", "w_in", "ln1_g", "mla_q_norm_g", "mla_w_uq", "mla_kv_norm_g", "mla_w_ukv", "diff_lambda", "diff_subln_g",
         "w_o", "ln2_g", "w_up", "w_down", "final_g", "positions_2", "norm_g_2", "ret_w_in_2", "ret_gn_g_2",
         "ret_w_out_2", "cf_w_pw1_2", "cf_b_pw1_2", "cf_w_dw_2", "cf_b_dw_2", "cf_ln_g_2", "cf_ln_b_2", "cf_w_pw2_2",
         "cf_b_pw2_2", "sc_w_in_2", "sc_w_conv_2", "sc_w_out_2", "mlp_w1_2", "mlp_w2_2")


def constants():
    import numpy as np
    f = np.float32
    tok = np.arange(S)

    def tables(dim):
        half = dim // 2
        inv = (f(1.0) / (f(10000.0) ** (np.arange(half, dtype=f) / f(half)))).astype(f)
        ang = tok.astype(f)[:, None] * inv[None, :]
        return np.cos(ang).astype(f), np.sin(ang).astype(f)

    rope = np.concatenate([*tables(AD), *tables(CQ)], axis=1).reshape(NT, P, 96).transpose(1, 0, 2)
    dist = tok[:, None] - tok[None, :]
    causal = dist >= 0
    seen = (causal & (dist <= 128)).astype(int) + (causal & (dist % 4 == 0)) + (causal & (dist % 16 == 0))
    dil = np.where(seen > 0, np.log(np.maximum(seen, 1)) * AD ** 0.5, -1e30)
    cau = np.where(causal, 0.0, -1e30)
    masks = np.stack([np.concatenate([m[:P, :P], m[P:, :]], axis=1) for m in (dil, cau)], axis=1)
    lg = np.log1p(-np.exp2(-5.0 - np.arange(RH)))
    dec = [np.where(causal.T, np.exp(g * np.maximum(dist.T, 0)), 0.0) * RDK ** -0.5 for g in lg]
    decay = np.concatenate([np.concatenate([m[:P, :], m[P:, P:]], axis=1) for m in dec], axis=1)
    inv = f(10000.0) ** (-np.arange(0, RDK, 2, dtype=f) / f(RDK))
    return {"c_ident": np.eye(P, dtype=f), "c_rope": np.ascontiguousarray(rope, dtype=f),
            "c_masks": np.ascontiguousarray(masks, dtype=f), "c_invfreq": inv.astype(f)[None],
            "c_decay": np.ascontiguousarray(decay, dtype=f)}


def kernel(**inputs):
    import numpy as np
    import concourse.bacc as bacc
    from concourse.bass_utils import run_bass_kernel_spmd

    nc = bacc.Bacc("TRN2", target_bir_lowering=False, num_devices=1)
    arrays, aps = {}, {}
    for name, v in [(n, inputs[n]) for n in NAMES] + list(constants().items()):
        v = np.ascontiguousarray(v)
        arrays[name + "_dram"] = v
        aps[name] = nc.dram_tensor(name + "_dram", v.shape, mybir.dt.from_np(v.dtype), kind="ExternalInput").ap()
    out = nc.dram_tensor("out_dram", (1, S, D), F32, kind="ExternalOutput").ap()
    build(nc, aps, out)
    r = run_bass_kernel_spmd(nc, [arrays], core_ids=[0])
    return r.results[0]["out_dram"]
```
